# Optimizing a Trainium2 kernel written in Bass

```python
import jax, jax.numpy as jnp
from jax import lax
import numpy as np

D_MODEL = 1024
BATCH = 1
SEQ = 1024
DEPTH = 1

HEAD_DIM = 64
N_Q_HEADS = D_MODEL // HEAD_DIM
N_KV_HEADS = N_Q_HEADS // 4
GQA_GROUP = N_Q_HEADS // N_KV_HEADS
ATTN_WIDTH = N_Q_HEADS * HEAD_DIM
KV_WIDTH = N_KV_HEADS * HEAD_DIM
WINDOW = 128
BLOCK = 128
CONV_WIDTH = D_MODEL
CONV_K = 3
D_FF = -(-8 * D_MODEL // (3 * 256)) * 256
SPLIT_SIZES = (ATTN_WIDTH, KV_WIDTH, KV_WIDTH, CONV_WIDTH, CONV_WIDTH, CONV_WIDTH, D_MODEL, D_MODEL)
IN_WIDTH = sum(SPLIT_SIZES)
SPLIT_POINTS = np.cumsum(SPLIT_SIZES)[:-1].tolist()
ALPHA = (2.0 * DEPTH) ** 0.25
BETA = (8.0 * DEPTH) ** -0.25
LN_EPS = 1e-5
NEG_INF = -1e30

kernel_name = "hybrid_shortconv_swa_sink_alibi_deepnorm"

def layer_norm(x, g, b):
    xf = x.astype(jnp.float32)
    mu = jnp.mean(xf, axis=-1, keepdims=True)
    var = jnp.mean(jnp.square(xf - mu), axis=-1, keepdims=True)
    y = (xf - mu) * lax.rsqrt(var + LN_EPS) * g.astype(jnp.float32) + b.astype(jnp.float32)
    return y.astype(x.dtype)

def alibi_slopes(n_heads):
    return np.array([2.0 ** (-8.0 * (i + 1) / n_heads) for i in range(n_heads)], dtype=np.float32)

def short_conv_mixer(b_gate, c_gate, h, conv_w):
    u = c_gate * h
    rhs = conv_w[:, None, :].astype(u.dtype)
    y = lax.conv_general_dilated(u, rhs, window_strides=(1,), padding=[(CONV_K - 1, 0)],
                                 dimension_numbers=('NWC', 'WIO', 'NWC'),
                                 feature_group_count=CONV_WIDTH)
    return b_gate * y

def sliding_window_attention(q, k, v, sinks):
    bsz, seq = q.shape[0], q.shape[1]
    nblk = seq // BLOCK
    qb = q.reshape(bsz, nblk, BLOCK, N_KV_HEADS, GQA_GROUP, HEAD_DIM)

    def band(t):
        tb = t.reshape(bsz, nblk, BLOCK, N_KV_HEADS, HEAD_DIM)
        prev = jnp.pad(tb[:, :-1], ((0, 0), (1, 0), (0, 0), (0, 0), (0, 0)))
        return jnp.concatenate([prev, tb], axis=2)

    kb, vb = band(k), band(v)
    scores = jnp.einsum('bnqkgd,bnskd->bnkgqs', qb, kb).astype(jnp.float32) * (HEAD_DIM ** -0.5)

    qi = np.arange(BLOCK)[:, None]
    kj = np.arange(2 * BLOCK)[None, :]
    dist = BLOCK + qi - kj
    in_window = (dist >= 0) & (dist < WINDOW)
    key_pos = (np.arange(nblk)[:, None] - 1) * BLOCK + np.arange(2 * BLOCK)[None, :]
    valid = in_window[None] & (key_pos >= 0)[:, None, :]
    slopes = alibi_slopes(N_Q_HEADS).reshape(N_KV_HEADS, GQA_GROUP)
    bias = -slopes[:, :, None, None] * np.abs(dist).astype(np.float32)[None, None]

    scores = jnp.where(valid[None, :, None, None], scores + bias, NEG_INF)
    sink = sinks.astype(jnp.float32).reshape(N_KV_HEADS, GQA_GROUP)[:, :, None, None]
    m = jnp.maximum(jnp.max(scores, axis=-1, keepdims=True), sink)
    p = jnp.exp(scores - m)
    probs = p / (jnp.sum(p, axis=-1, keepdims=True) + jnp.exp(sink - m))
    out = jnp.einsum('bnkgqs,bnskd->bnqkgd', probs.astype(v.dtype), vb)
    return out.reshape(bsz, seq, ATTN_WIDTH)

def setup_inputs(seed: int = 0) -> dict:
    key = jax.random.key(seed)
    ks = jax.random.split(key, 13)
    f32 = jnp.float32
    x = jax.random.normal(ks[0], (BATCH, SEQ, D_MODEL), f32)
    w_in = jax.random.normal(ks[1], (DEPTH, D_MODEL, IN_WIDTH), f32) * D_MODEL ** -0.5
    conv_w = jax.random.normal(ks[2], (DEPTH, CONV_K, CONV_WIDTH), f32) * CONV_K ** -0.5
    attn_sinks = jax.random.normal(ks[3], (DEPTH, N_Q_HEADS), f32) * 0.5
    w_out = jax.random.normal(ks[4], (DEPTH, D_MODEL, D_MODEL), f32) * (D_MODEL ** -0.5 * BETA)
    ln1_g = 1.0 + 0.02 * jax.random.normal(ks[5], (DEPTH, D_MODEL), f32)
    ln1_b = 0.02 * jax.random.normal(ks[6], (DEPTH, D_MODEL), f32)
    w_gate = jax.random.normal(ks[7], (DEPTH, D_MODEL, D_FF), f32) * D_MODEL ** -0.5
    w_up = jax.random.normal(ks[8], (DEPTH, D_MODEL, D_FF), f32) * D_MODEL ** -0.5
    w_down = jax.random.normal(ks[9], (DEPTH, D_FF, D_MODEL), f32) * (D_FF ** -0.5 * BETA)
    ln2_g = 1.0 + 0.02 * jax.random.normal(ks[10], (DEPTH, D_MODEL), f32)
    ln2_b = 0.02 * jax.random.normal(ks[11], (DEPTH, D_MODEL), f32)
    return {"x": x, "w_in": w_in, "conv_w": conv_w, "attn_sinks": attn_sinks, "w_out": w_out,
            "ln1_g": ln1_g, "ln1_b": ln1_b, "w_gate": w_gate, "w_up": w_up, "w_down": w_down,
            "ln2_g": ln2_g, "ln2_b": ln2_b}

def reference(x, w_in, conv_w, attn_sinks, w_out, ln1_g, ln1_b, w_gate, w_up, w_down, ln2_g, ln2_b):
    bsz, seq = x.shape[0], x.shape[1]
    for l in range(DEPTH):
        proj = jnp.einsum('bsd,de->bse', x, w_in[l])
        q, k, v, cb, cc, ch, g_conv, g_attn = jnp.split(proj, SPLIT_POINTS, axis=-1)
        y_conv = short_conv_mixer(cb, cc, ch, conv_w[l])
        y_attn = sliding_window_attention(q, k, v, attn_sinks[l])
        merged = jax.nn.sigmoid(g_conv) * y_conv + jax.nn.sigmoid(g_attn) * y_attn
        mix = jnp.einsum('bse,ed->bsd', merged, w_out[l])
        x = layer_norm(ALPHA * x + mix, ln1_g[l], ln1_b[l])
        hid = jax.nn.silu(jnp.einsum('bsd,df->bsf', x, w_gate[l])) * jnp.einsum('bsd,df->bsf', x, w_up[l])
        ffn = jnp.einsum('bsf,fd->bsd', hid, w_down[l])
        x = layer_norm(ALPHA * x + ffn, ln2_g[l], ln2_b[l])
    return x.reshape(bsz, seq, D_MODEL)


_drawn_inputs = setup_inputs


def setup_inputs(seed=0):
    import zlib

    import numpy as np

    out = dict(_drawn_inputs(seed))
    spreads = {}
    factors = {'attn_sinks': 7.906, 'ln2_g': 2.923, 'ln2_b': 2.83}
    for name, (base, spread) in spreads.items():
        noise = np.random.default_rng([zlib.crc32(name.encode()), seed]).standard_normal(out[name].shape)
        drawn = base * np.exp(spread * noise) if base else spread * noise
        out[name] = __import__('jax').numpy.asarray(drawn.astype(out[name].dtype))
    for name, factor in factors.items():
        out[name] = (out[name] * factor).astype(out[name].dtype)
    return out
```

```python
from contextlib import ExitStack

import numpy as np

import concourse.bass as bass
from concourse import mybir

F32 = mybir.dt.float32
F32R = mybir.dt.float32r
ALU = mybir.AluOpType
ACT = mybir.ActivationFunctionType
AX_X = mybir.AxisListType.X

P = 128
D = 1024
S = 1024
DT = D // P
HALF = 512
HD = 64
NQ, NKV = 16, 4
G = NQ // NKV
NB = S // P
DFF = 2816
FT = DFF // P
NG = FT // 2
ALPHA = 2.0 ** 0.25
EPS = 1e-5
NEG = -1e30
SCALE = HD ** -0.5

COL_Q, COL_K, COL_V = 0, D, D + NKV * HD
COL_CB = COL_V + NKV * HD
COL_CC, COL_CH, COL_GC, COL_GA = (COL_CB + D * n for n in (1, 2, 3, 4))

PRO_TILES = 4
TILES = [("q", 0), ("q", 1), ("ga", 0), ("ga", 1)] + [(x, j) for j in (0, 1) for x in ("cc", "ch", "cb", "gc")]
NT = len(TILES)
IN_TILES = PRO_TILES + NKV * NT
OUT_TILES = 2 * DT
COLS = {"q": COL_Q, "ga": COL_GA, "cc": COL_CC, "ch": COL_CH, "cb": COL_CB, "gc": COL_GC}


def head_schedule():
    first = 4
    steps = []
    for u in range(2 * NT):
        v = u - first
        if v >= 2 and v % 2 == 0 and (v - 2) // 2 < NB:
            steps.append(("scores", (v - 2) // 2))
        steps.append(("unit", u))
        if v >= 3 and v % 2 == 1 and (v - 3) // 2 < NB:
            steps.append(("turn", (v - 3) // 2))
        if v >= 4 and v % 2 == 0 and (v - 4) // 2 < NB:
            steps.append(("values", (v - 4) // 2))
    return steps


STEPS = head_schedule()

SOFT = 8


def turned(n, kb):
    return 0 if n == 0 else 2 * n - 1 + kb


NTURN = 2 * NB - 1


def build(nc, x, w_in, conv_w, sinks, w_out, ln1_g, ln1_b, w_gate, w_up, w_down, ln2_g, ln2_b, out):
    ctx = ExitStack()
    with ctx:
        def sem(name):
            return ctx.enter_context(nc.semaphore(name))

        def sb(stack, name, shape, dt=F32):
            return stack.enter_context(nc.sbuf_tensor(name, shape, dt))

        act_hi = sb(ctx, "act_hi", [P, DT, S], F32R)
        act_lo = sb(ctx, "act_lo", [P, DT, S], F32R)
        res = sb(ctx, "res", [P, DT, S])
        raw = sb(ctx, "raw", [P, 2, DT, P])
        w_hi = sb(ctx, "w_hi", [P, 2, DT, P], F32R)
        w_lo = sb(ctx, "w_lo", [P, 2, DT, P], F32R)
        ident = sb(ctx, "ident", [P, P])
        mean_of = sb(ctx, "mean_of", [P, P])
        cw = sb(ctx, "cw", [P, DT, 3])
        snk = sb(ctx, "snk", [P, NQ])
        lng = sb(ctx, "lng", [P, 2, DT])
        lnb = sb(ctx, "lnb", [P, 2, DT])
        eps = sb(ctx, "eps", [P, 1])

        with ExitStack() as st:
            q_st = sb(st, "q_st", [P, G, S], F32R)
            pt_hi = sb(st, "pt_hi", [P, 2, G * P], F32R)
            pt_lo = sb(st, "pt_lo", [P, 2, G * P], F32R)
            prob = sb(st, "prob", [P, G, 2 * P])
            tga = sb(st, "tga", [P, 2, S])
            ks_hi = sb(st, "ks_hi", [P, S], F32R)
            ks_lo = sb(st, "ks_lo", [P, S], F32R)
            vs = sb(st, "vs", [P, NB, 2 * HD], F32R)
            bias = sb(st, "bias", [P, G, 2 * P])
            negdist = sb(st, "negdist", [P, 2 * P])
            mask = sb(st, "mask", [P, 2 * P])
            slope = sb(st, "slope", [P, G])
            snkc = sb(st, "snkc", [P, G])
            cwc = sb(st, "cwc", [P, 2, 3])
            ccs = sb(st, "ccs", [P, S])
            u_pad = sb(st, "u_pad", [P, 2 + S])
            yc = sb(st, "yc", [P, S])
            tgc = sb(st, "tgc", [P, S])
            o_lo = sb(st, "o_lo", [HD, G * P])
            o_sum = sb(st, "o_sum", [P, 2, P])
            mx = sb(st, "mx", [P, G])
            neg_m = sb(st, "neg_m", [P, G])
            sink_d = sb(st, "sink_d", [P, G])
            sink_e = sb(st, "sink_e", [P, G])
            rsum = sb(st, "rsum", [P, G])
            rden = sb(st, "rden", [P, G])
        with ExitStack() as st:
            xs = sb(st, "xs", [P, NB, D])

        late = ctx.enter_context(ExitStack())
        acc = sb(late, "acc", [P, HALF])
        acc2 = sb(late, "acc2", [P, HALF])
        rstd = sb(late, "rstd", [P, HALF])
        sq = sb(late, "sq", [P, 2, HALF])
        raw_b = sb(late, "raw_b", [P, 2, DT, P])
        with ExitStack() as st:
            m_hi, m_lo = [], []
            for h in range(2):
                m_hi.append(sb(st, f"m_hi{h}", [P, DT, HALF], F32R))
                m_lo.append(sb(st, f"m_lo{h}", [P, DT, HALF], F32R))
        with ExitStack() as st:
            w_hi_b = sb(st, "w_hi_b", [P, 2, DT, P], F32R)
            w_lo_b = sb(st, "w_lo_b", [P, 2, DT, P], F32R)
            wd_hi = sb(st, "wd_hi", [P, 2, D], F32R)
            wd_lo = sb(st, "wd_lo", [P, 2, D], F32R)
            raw_d = sb(st, "raw_d", [P, 2, D])
            hid_hi = sb(st, "hid_hi", [P, 2, S], F32R)
            hid_lo = sb(st, "hid_lo", [P, 2, S], F32R)
            tanh_g = sb(st, "tanh_g", [P, 2, HALF])
            hid = sb(st, "hid", [P, 2, HALF])
        with ExitStack() as st:
            ost = sb(st, "ost", [P, 2, D])

        ps = ctx.enter_context(nc.psum_tensor("ps", [P, 8, HALF], F32))
        SCORE, TURN, OUT = 3, 5, 7
        scores_ps = ps[:, SCORE:SCORE + 2, :].rearrange("p b (g k) -> p (b g) k", k=2 * P)

        x_in = [sem(f"x_in{i}") for i in range(NB)]
        params_in = sem("params_in")
        w_in_s = [sem(f"w_landed{i}") for i in range(2)]
        tables = sem("tables")
        x_turned, x_hi_s, x_lo_s = sem("x_turned"), sem("x_hi_done"), sem("x_lo_done")
        w_hi_s, w_lo_s = sem("w_hi_done"), sem("w_lo_done")
        unit_s = sem("unit_done")
        k_copied, v_copied, v_turned, v_kept = sem("k_copied"), sem("v_copied"), sem("v_turned"), sem("v_kept")
        prep_act, prep_dve = sem("head_prep_act"), sem("head_prep_dve")
        q_hi_s, q_lo_s = sem("q_hi_done"), sem("q_lo_done")
        ga_s, cc_s, gc_s = sem("ga_tanh_done"), sem("cc_copied"), sem("gc_tanh_done")
        conv_s = sem("conv_step")
        scores_s, soft_s, exp_s = sem("scores_done"), sem("softmax_step"), sem("exp_done")
        turn_s, pt_hi_s, pt_lo_s = sem("probs_turned"), sem("pt_hi_done"), sem("pt_lo_done")
        values_s, olo_s, o_s = sem("values_done"), sem("o_lo_copied"), sem("o_step")
        merge_s = sem("merge_done")
        m_hi_s, m_lo_s, xsum_s = sem("m_hi_done"), sem("m_lo_done"), sem("x_sum_done")
        out_s, res_s = sem("out_unit_done"), sem("res_tile_done")
        acc_s, stat_s, cen_s, sq_s, sqacc_s = (sem("channel_sum_step"), sem("stat_done"), sem("centred"),
                                               sem("squared"), sem("square_sum_step"))
        std_s, rstd_s, norm_s, aff_s = sem("std_done"), sem("rstd_done"), sem("normalised"), sem("affine_done")
        n_hi_s, n_lo_s, scaled_s = sem("norm_hi_done"), sem("norm_lo_done"), sem("residual_scaled")
        fw_in = [sem(f"ffn_w_landed{i}") for i in range(6)]
        fw_hi_s, fw_lo_s = sem("ffn_w_hi_done"), sem("ffn_w_lo_done")
        f_s, d_s = sem("gate_up_unit_done"), sem("down_unit_done")
        silu_s, hid_s, add_s = sem("silu_act_step"), sem("hidden_step"), sem("down_added")
        ot_s, ocp_act, ocp_dve = sem("out_turned"), sem("out_copied_act"), sem("out_copied_dve")
        stored = [sem(f"stored{i}") for i in range(2)]

        block = ctx.enter_context(nc.Block())

        def half(h):
            return slice(h * HALF, (h + 1) * HALF)

        def blk(n):
            return slice(n * P, (n + 1) * P)

        def fp(ap):
            return ap.bitcast(F32)

        def unit_bank(u):
            return u % 3

        def consumed(k, u):
            kind, j = TILES[u // 2]
            h = u % 2
            if kind == "q":
                return q_lo_s, 8 * k + 4 * j + 2 * h + 2
            if kind == "ga":
                return ga_s, 4 * k + 2 * j + h + 1
            if kind == "cc":
                return cc_s, 4 * k + 2 * j + h + 1
            if kind == "gc":
                return gc_s, 4 * k + 2 * j + h + 1
            return conv_s, 24 * k + 12 * j + (4 * h + 1 if kind == "ch" else 9 + h)

        def ffn_raw(s):
            return raw_b[:, s] if s < 2 else raw[:, s - 2] if s < 4 else raw_d[:, s - 4]

        def ffn_hi(s):
            return w_hi_b[:, s] if s < 2 else w_hi[:, s - 2] if s < 4 else wd_hi[:, s - 4]

        def ffn_lo(s):
            return w_lo_b[:, s] if s < 2 else w_lo[:, s - 2] if s < 4 else wd_lo[:, s - 4]

        def stat_bank(q, which):
            return (6 if q < 2 else 0) + which

        @block.sync
        def _(sp):
            def load_w(tile_slot, w, col):
                src = w[0, :, bass.ds(col, P)].rearrange("(t p) c -> p t c", p=P)
                sp.dma_start(raw[:, tile_slot], src).then_inc(w_in_s[tile_slot], 16)

            for i in range(4):
                sp.dma_start(xs[:, i, :], x[0, blk(i), :]).then_inc(x_in[i], 16)
            load_w(0, w_in, COL_K)
            for i in range(4, NB):
                sp.dma_start(xs[:, i, :], x[0, blk(i), :]).then_inc(x_in[i], 16)
            load_w(1, w_in, COL_K + P)
            with nc.allow_non_contiguous_dma(reason="per-channel parameters, loaded once"):
                sp.dma_start(snk[:], sinks[0:1, :].partition_broadcast(P)).then_inc(params_in, 16)
                for t in range(3):
                    sp.dma_start(cw[:, :, t], conv_w[0, t].rearrange("(m p) -> p m", p=P)).then_inc(params_in, 16)
                for dst, srcs in ((lng, (ln1_g, ln2_g)), (lnb, (ln1_b, ln2_b))):
                    for n in range(2):
                        sp.dma_start(dst[:, n, :], srcs[n][0].rearrange("(m p) -> p m", p=P)).then_inc(params_in, 16)
            for t in (2, 3):
                sp.wait_ge(w_lo_s, t - 1)
                load_w(t % 2, w_in, COL_V + P * (t - 2))
            with sp.Fori(0, NKV) as k:
                for i, (kind, j) in enumerate(TILES):
                    sp.wait_ge(w_lo_s, k * NT + (PRO_TILES + i - 1))
                    load_w(i % 2, w_in, k * (2 * P) + (COLS[kind] + P * j))
            def load_ffn(g, s):
                if s < 4:
                    w = (w_gate, w_up)[s % 2]
                    src = w[0, :, bass.ds(g * (2 * P) + P * (s // 2), P)].rearrange("(t p) c -> p t c", p=P)
                else:
                    src = w_down[0, bass.ds(g * (2 * P) + P * (s - 4), P), :]
                sp.dma_start(ffn_raw(s), src).then_inc(fw_in[s], 16)

            for v in range(OUT_TILES):
                sp.wait_ge(w_lo_s, IN_TILES + v - 1)
                load_w(v % 2, w_out, P * (v % DT))
                if v == DT:
                    sp.wait_ge(merge_s, 2 * NKV)
                    load_ffn(0, 0)
                    load_ffn(0, 1)
            for s in (2, 3):
                sp.wait_ge(w_lo_s, IN_TILES + OUT_TILES - 3 + s)
                load_ffn(0, s)
            sp.wait_ge(out_s, OUT_TILES)
            load_ffn(0, 4)
            load_ffn(0, 5)
            with sp.Fori(1, NG) as g:
                for s in range(6):
                    sp.wait_ge(fw_lo_s, g * 6 + (s - 5))
                    load_ffn(g, s)
            for i in range(NB):
                sp.wait_ge(ocp_act, i + 1)
                sp.wait_ge(ocp_dve, i + 1)
                sp.dma_start(out[0, blk(i), :], ost[:, i % 2, :]).then_inc(stored[i % 2], 16)
            for i in range(2):
                sp.wait_ge(stored[i], 16 * NB // 2)

        @block.gpsimd
        def _(pool):
            pool.memset(ident[:], 0.0).then_inc(tables, 1)
            pool.wait_ge(tables, 1)
            pool.affine_select(out=ident[:], in_=ident[:], compare_op=ALU.not_equal, fill=1.0, base=0,
                               pattern=[[-1, P]], channel_multiplier=1).then_inc(tables, 1)
            pool.memset(mean_of[:], 1.0 / D).then_inc(tables, 1)
            pool.memset(eps[:], EPS).then_inc(tables, 1)
            pool.memset(u_pad[:, 0:2], 0.0).then_inc(tables, 1)
            pool.iota(negdist[:], pattern=[[1, 2 * P]], base=-P, channel_multiplier=-1,
                      allow_small_or_imprecise_dtypes=True).then_inc(tables, 1)
            pool.memset(mask[:], 0.0).then_inc(tables, 1)
            pool.wait_ge(tables, 7)
            pool.affine_select(out=mask[:], in_=mask[:], compare_op=ALU.is_ge, fill=NEG, base=P,
                               pattern=[[-1, 2 * P]], channel_multiplier=1).then_inc(tables, 1)
            pool.wait_ge(tables, 8)
            pool.affine_select(out=mask[:], in_=mask[:], compare_op=ALU.is_ge, fill=NEG, base=-1,
                               pattern=[[1, 2 * P]], channel_multiplier=-1).then_inc(tables, 1)
            for g in range(G):
                pool.memset(slope[:, g:g + 1], float(np.float32(2.0 ** (-8.0 * (g + 1) / NQ)))).then_inc(tables, 1)

            def low_part(count, slot):
                pool.wait_ge(w_hi_s, count)
                pool.tensor_tensor(w_lo[:, slot], raw[:, slot], fp(w_hi[:, slot]), ALU.subtract).then_inc(w_lo_s, 1)

            for t in range(6):
                low_part(t + 1, t % 2)
            with pool.Fori(0, NKV) as k:
                for i in range(NT):
                    low_part(k * NT + (6 + i + 1), i % 2)

            def ffn_low_part(g, s):
                pool.wait_ge(fw_hi_s, g * 6 + (s + 1))
                pool.tensor_tensor(ffn_lo(s), ffn_raw(s), fp(ffn_hi(s)), ALU.subtract).then_inc(fw_lo_s, 1)

            def channel_sum(q, m, ready, count):
                if m == 0:
                    return
                pool.wait_ge(ready, count)
                first = res[:, 0, half(q % 2)] if m == 1 else acc[:]
                if m == 1:
                    if q:
                        pool.wait_ge(stat_s, 2 * q - 1)
                else:
                    pool.wait_ge(acc_s, 7 * q + m - 1)
                pool.tensor_tensor(acc[:], first, res[:, m, half(q % 2)], ALU.add).then_inc(acc_s, 1)

            def square_sum(q):
                for m in range(1, DT):
                    pool.wait_ge(sq_s, 8 * q + m + 1)
                    if m == 1:
                        if q:
                            pool.wait_ge(stat_s, 2 * q)
                        pool.tensor_tensor(acc2[:], sq[:, 0], sq[:, 1], ALU.add).then_inc(sqacc_s, 1)
                    else:
                        pool.wait_ge(sqacc_s, 7 * q + m - 1)
                        pool.tensor_tensor(acc2[:], acc2[:], sq[:, m % 2], ALU.add).then_inc(sqacc_s, 1)

            for v in range(OUT_TILES):
                if v + 2 < OUT_TILES:
                    low_part(IN_TILES + v + 3, v % 2)
                if v in (9, 10):
                    ffn_low_part(0, v - 9)
                channel_sum(v // DT, v % DT, res_s, 2 + v + 1)
                if v == DT + 1:
                    square_sum(0)
            ffn_low_part(0, 2)
            ffn_low_part(0, 3)
            square_sum(1)
            ffn_low_part(0, 4)
            ffn_low_part(0, 5)
            with pool.Fori(1, NG) as g:
                for s in range(6):
                    ffn_low_part(g, s)
            for q in (2, 3):
                for m in range(DT):
                    channel_sum(q, m, add_s, 16 * (NG - 1) + DT * (q - 2) + m + 1)
                square_sum(q)

        @block.scalar
        def _(act):
            def high_part(landed, slot, free, count):
                act.wait_ge(w_in_s[slot], landed)
                if free is not None:
                    act.wait_ge(free, count)
                act.activation(w_hi[:, slot], raw[:, slot], ACT.Copy).then_inc(w_hi_s, 1)

            def x_high(i):
                act.wait_ge(x_turned, i + 1)
                st, cg = i // 2, i % 2
                act.activation(act_hi[:, 4 * cg:4 * cg + 4, blk(st)],
                               ps[:, 4 + i % 4, :].rearrange("p (c s) -> p c s", c=4), ACT.Copy).then_inc(x_hi_s, 1)

            for i in range(8):
                x_high(i)
            high_part(16, 0, None, 0)
            for i in range(8, 16):
                x_high(i)
            high_part(16, 1, None, 0)
            for n in range(2 * PRO_TILES):
                t, h = n // 2, n % 2
                act.wait_ge(unit_s, n + 1)
                bank = ps[:, unit_bank(n + 1), :]
                if t < 2:
                    act.wait_ge(x_lo_s, 16)
                    for e in range(2):
                        for to in range(2):
                            act.activation(res[to * HD:(to + 1) * HD, 2 * (2 * t + e), half(h)],
                                           bank[e * HD:(e + 1) * HD, :], ACT.Copy).then_inc(k_copied, 1)
                else:
                    i = n - 4
                    if i >= 2:
                        act.wait_ge(v_turned, i - 1)
                    act.activation(yc[:, half(i % 2)], bank, ACT.Copy).then_inc(v_copied, 1)
                if h == 1:
                    high_part(16 * ((t + 2) // 2 + 1), t % 2, unit_s, n + 1)

            act.wait_ge(v_kept, 8)
            with act.Fori(0, NKV) as k:
                act.activation(ks_hi[:], res[:, bass.ds(k * 2, 1), :].rearrange("p a s -> p (a s)"), ACT.Copy).then_inc(prep_act, 1)
                act.activation(vs[:, :, 0:HD],
                               res[:, bass.ds(k * 2 + 1, 1), 0:NB * HD].rearrange("p a (b d) -> p (a b) d", b=NB),
                               ACT.Copy).then_inc(prep_act, 1)
                for step, n in STEPS:
                    if step == "unit":
                        kind, j = TILES[n // 2]
                        h = n % 2
                        bank = ps[:, unit_bank(n), :]
                        done = k * (2 * NT) + (2 * PRO_TILES + n + 1)
                        if kind in ("q", "ga", "cc", "gc"):
                            act.wait_ge(unit_s, done)
                        if kind == "q":
                            for e in range(2):
                                rows = slice(e * HD, (e + 1) * HD)
                                act.activation(q_st[rows, 2 * j + e, half(h)], bank[rows, :],
                                               ACT.Copy).then_inc(q_hi_s, 1)
                        elif kind == "ga":
                            act.activation(tga[:, j, half(h)], bank, ACT.Tanh, scale=0.5).then_inc(ga_s, 1)
                        elif kind == "cc":
                            if j:
                                act.wait_ge(conv_s, k * 24 + 12)
                            act.activation(ccs[:, half(h)], bank, ACT.Copy).then_inc(cc_s, 1)
                        elif kind == "gc":
                            if j:
                                act.wait_ge(conv_s, k * 24 + 12)
                            act.activation(tgc[:, half(h)], bank, ACT.Tanh, scale=0.5).then_inc(gc_s, 1)
                        if h == 1:
                            i = n // 2
                            high_part(k * (16 * NT // 2) + 16 * ((PRO_TILES + i + 2) // 2 + 1), i % 2, unit_s, done)
                    elif step == "scores":
                        lo = P if n == 0 else 0
                        act.wait_ge(soft_s, k * (SOFT * NB) + (SOFT * n + 5))
                        act.activation(sink_e[:], sink_d[:], ACT.Exp).then_inc(exp_s, 1)
                        for g in range(G):
                            act.activation(prob[:, g, lo:], prob[:, g, lo:], ACT.Exp, bias=neg_m[:, g:g + 1],
                                           accum_out=rsum[:, g:g + 1]).then_inc(exp_s, 1)
                    elif step == "turn":
                        for kb in range(1 if n == 0 else 0, 2):
                            i = k * NTURN + (turned(n, kb) + 1)
                            act.wait_ge(turn_s, i)
                            act.activation(pt_hi[:, kb], ps[:, TURN + kb, :], ACT.Copy).then_inc(pt_hi_s, 1)
                    else:
                        act.wait_ge(values_s, k * NB + (n + 1))
                        if n:
                            act.wait_ge(o_s, k * (3 * NB) + 3 * n)
                        act.activation(o_lo[:], ps[HD:P, OUT, :], ACT.Copy).then_inc(olo_s, 1)
                act.wait_ge(merge_s, k * 2 + 2)

            for h in range(2):
                for m in range(DT):
                    act.activation(m_hi[h][:, m], res[:, m, half(h)], ACT.Copy, scale=0.5).then_inc(m_hi_s, 1)

            def ffn_high_part(g, s, free, count):
                act.wait_ge(fw_in[s], (g + 1) * 16)
                act.wait_ge(free, count)
                act.activation(ffn_hi(s), ffn_raw(s), ACT.Copy).then_inc(fw_hi_s, 1)

            def squares(q):
                for m in range(DT):
                    act.wait_ge(cen_s, 8 * q + m + 1)
                    if m >= 2:
                        act.wait_ge(sqacc_s, 7 * q + m - 1)
                    elif q:
                        act.wait_ge(sqacc_s, 7 * q)
                    act.activation(sq[:, m % 2], res[:, m, half(q % 2)], ACT.Square).then_inc(sq_s, 1)

            def root(q):
                act.wait_ge(stat_s, 2 * q + 2)
                if q:
                    act.wait_ge(norm_s, 8 * q)
                act.activation(rstd[:], ps[:, stat_bank(q, 1), :], ACT.Sqrt, bias=eps[:]).then_inc(std_s, 1)

            def affine(q, ms):
                for m in ms:
                    act.wait_ge(norm_s, 8 * q + m + 1)
                    tile = res[:, m, half(q % 2)]
                    act.activation(tile, tile, ACT.Identity, bias=lnb[:, q // 2, m:m + 1],
                                   scale=lng[:, q // 2, m:m + 1]).then_inc(aff_s, 1)
                    if q < 2:
                        act.wait_ge(aff_s, 8 * q + m + 1)
                        act.activation(act_hi[:, m, half(q)], tile, ACT.Copy).then_inc(n_hi_s, 1)

            act.wait_ge(params_in, 16 * 8)
            for v in range(OUT_TILES):
                if v + 2 < OUT_TILES:
                    t = IN_TILES + v + 2
                    high_part(16 * (t // 2 + 1), v % 2, out_s, v + 1)
                if v in (9, 10):
                    ffn_high_part(0, v - 9, out_s, DT)
                if v == DT + 1:
                    squares(0)
                if v == 11:
                    root(0)
                if v == 12:
                    affine(0, range(4))
                if v == 13:
                    affine(0, range(4, DT))
            ffn_high_part(0, 2, out_s, OUT_TILES - 1)
            ffn_high_part(0, 3, out_s, OUT_TILES)

            def silu(g, h, t):
                act.wait_ge(f_s, g * 8 + (4 * h + 2 * t + 1))
                if h:
                    act.wait_ge(hid_s, g * 12 + (3 * t + 1))
                act.activation(tanh_g[:, t], ps[:, 2 * t, :], ACT.Tanh, scale=0.5).then_inc(silu_s, 1)
                act.wait_ge(hid_s, g * 12 + (6 * h + 3 * t + 2))
                act.activation(hid_hi[:, t, half(h)], hid[:, t], ACT.Copy, scale=0.5).then_inc(silu_s, 1)

            squares(1)
            silu(0, 0, 0)
            root(1)
            affine(1, range(DT))
            silu(0, 0, 1)
            ffn_high_part(0, 4, out_s, OUT_TILES)
            ffn_high_part(0, 5, out_s, OUT_TILES)

            with act.Fori(0, NG - 1) as g:
                silu(g, 1, 0)
                silu(g, 1, 1)
                for s in range(4):
                    ffn_high_part(g + 1, s, f_s, g * 8 + 8)
                for s in (4, 5):
                    ffn_high_part(g + 1, s, d_s, g * 16 + 16)
                act.wait_ge(hid_s, g * 12 + 12)
                silu(g + 1, 0, 0)
                silu(g + 1, 0, 1)
            silu(NG - 1, 1, 0)
            silu(NG - 1, 1, 1)
            squares(2)
            root(2)
            squares(3)
            affine(2, range(DT))
            root(3)
            affine(3, range(DT))
            for i in range(NB):
                act.wait_ge(ot_s, 2 * i + 1)
                if i >= 2:
                    act.wait_ge(stored[i % 2], 16 * (i // 2))
                act.activation(ost[:, i % 2, 0:HALF], ps[:, 2 + 2 * (i % 3), :], ACT.Copy).then_inc(ocp_act, 1)

        @block.vector
        def _(dve):
            dve.wait_ge(tables, 13)
            for i in range(16):
                dve.wait_ge(x_hi_s, i + 1)
                st, cg = i // 2, i % 2
                dst = (slice(None), slice(4 * cg, 4 * cg + 4), blk(st))
                dve.tensor_tensor(act_lo[dst], ps[:, 4 + i % 4, :].rearrange("p (c s) -> p c s", c=4),
                                  fp(act_hi[dst]), ALU.subtract).then_inc(x_lo_s, 1)
            for i in range(4):
                j, h = i // 2, i % 2
                dve.wait_ge(v_turned, i + 1)
                src = ps[:, 3 + i % 2, :].rearrange("p (b e d) -> p e b d", b=4, e=2)
                for e in range(2):
                    dst = res[:, 2 * (2 * j + e) + 1, 4 * HD * h:4 * HD * (h + 1)].rearrange("p (b d) -> p b d", b=4)
                    dve.tensor_copy(dst, src[:, e]).then_inc(v_kept, 1)
            dve.wait_ge(params_in, 16 * 8)

            with dve.Fori(0, NKV) as k:
                def prep_done(n):
                    dve.wait_ge(prep_dve, k * 9 + n)

                dve.wait_ge(prep_act, k * 2 + 1)
                dve.tensor_tensor(ks_lo[:], res[:, bass.ds(k * 2, 1), :].rearrange("p a s -> p (a s)"),
                                  fp(ks_hi[:]), ALU.subtract).then_inc(prep_dve, 1)
                dve.wait_ge(prep_act, k * 2 + 2)
                dve.tensor_tensor(vs[:, :, HD:2 * HD],
                                  res[:, bass.ds(k * 2 + 1, 1), 0:NB * HD].rearrange("p a (b d) -> p (a b) d", b=NB),
                                  fp(vs[:, :, 0:HD]), ALU.subtract).then_inc(prep_dve, 1)
                for g in range(G):
                    dve.scalar_tensor_tensor(out=bias[:, g], in0=negdist[:], scalar=slope[:, g:g + 1], in1=mask[:],
                                             op0=ALU.mult, op1=ALU.add).then_inc(prep_dve, 1)
                prep_done(6)
                dve.tensor_scalar(slope[:], slope[:], 2.0 ** (-8.0 * G / NQ), None, ALU.mult).then_inc(prep_dve, 1)
                dve.tensor_copy(snkc[:], snk[:, bass.ds(k * G, G)]).then_inc(prep_dve, 1)
                dve.tensor_copy(cwc[:], cw[:, bass.ds(k * 2, 2), :]).then_inc(prep_dve, 1)
                prep_done(9)

                def conv_done(j, n):
                    if 12 * j + n:
                        dve.wait_ge(conv_s, k * 24 + (12 * j + n))

                def unit(n):
                    kind, j = TILES[n // 2]
                    h = n % 2
                    bank = ps[:, unit_bank(n), :]
                    done = k * (2 * NT) + (2 * PRO_TILES + n + 1)
                    cols = half(h)
                    if kind == "q":
                        for e in range(2):
                            rows, other = slice(e * HD, (e + 1) * HD), slice((1 - e) * HD, (2 - e) * HD)
                            dve.wait_ge(q_hi_s, k * 8 + (4 * j + 2 * h + 2))
                            dve.tensor_tensor(q_st[other, 2 * j + e, cols], bank[rows, :],
                                              fp(q_st[rows, 2 * j + e, cols]), ALU.subtract).then_inc(q_lo_s, 1)
                    elif kind == "ch":
                        dve.wait_ge(unit_s, done)
                        dve.wait_ge(cc_s, k * 4 + (2 * j + h + 1))
                        conv_done(j, 4 * h)
                        dve.tensor_tensor(u_pad[:, 2 + h * HALF:2 + (h + 1) * HALF], bank, ccs[:, cols],
                                          ALU.mult).then_inc(conv_s, 1)
                        conv_done(j, 4 * h + 1)
                        dve.tensor_scalar(yc[:, cols], u_pad[:, h * HALF:(h + 1) * HALF], cwc[:, j, 0:1], None,
                                          ALU.mult).then_inc(conv_s, 1)
                        for t in (1, 2):
                            conv_done(j, 4 * h + 1 + t)
                            dve.scalar_tensor_tensor(out=yc[:, cols], in0=u_pad[:, h * HALF + t:(h + 1) * HALF + t],
                                                     scalar=cwc[:, j, t:t + 1], in1=yc[:, cols], op0=ALU.mult,
                                                     op1=ALU.add).then_inc(conv_s, 1)
                    elif kind == "cb":
                        dve.wait_ge(unit_s, done)
                        conv_done(j, 8 + h)
                        dve.tensor_tensor(yc[:, cols], bank, yc[:, cols], ALU.mult).then_inc(conv_s, 1)
                    elif kind == "gc":
                        dve.wait_ge(gc_s, k * 4 + (2 * j + h + 1))
                        conv_done(j, 10 + h)
                        dve.scalar_tensor_tensor(out=res[:, bass.ds(k * 2 + j, 1), cols].rearrange("p a s -> p (a s)"),
                                                 in0=tgc[:, cols], scalar=1.0, in1=yc[:, cols], op0=ALU.add,
                                                 op1=ALU.mult).then_inc(conv_s, 1)
                        if j == 1:
                            conv_done(1, 11 + h)
                            dve.wait_ge(o_s, k * (3 * NB) + (3 * NB if h else 3 * NB // 2))
                            both = res[:, bass.ds(k * 2, 2), cols]
                            dve.tensor_tensor(both, both, tga[:, :, cols], ALU.add).then_inc(merge_s, 1)

                def soft_done(n, step):
                    if SOFT * n + step:
                        dve.wait_ge(soft_s, k * (SOFT * NB) + (SOFT * n + step))

                def softmax(n):
                    lo = P if n == 0 else 0
                    dve.wait_ge(scores_s, k * NB + (n + 1))
                    soft_done(n, 0)
                    dve.scalar_tensor_tensor(out=prob[:, :, lo:], in0=scores_ps[:, :, lo:], scalar=SCALE,
                                             in1=bias[:, :, lo:], op0=ALU.mult, op1=ALU.add).then_inc(soft_s, 1)
                    soft_done(n, 1)
                    dve.tensor_reduce(mx[:], prob[:, :, lo:], AX_X, ALU.max).then_inc(soft_s, 1)
                    soft_done(n, 2)
                    dve.tensor_tensor(mx[:], mx[:], snkc[:], ALU.max).then_inc(soft_s, 1)
                    soft_done(n, 3)
                    dve.tensor_scalar(neg_m[:], mx[:], -1.0, None, ALU.mult).then_inc(soft_s, 1)
                    dve.tensor_tensor(sink_d[:], snkc[:], mx[:], ALU.subtract).then_inc(soft_s, 1)

                def normalise(n):
                    lo = P if n == 0 else 0
                    dve.wait_ge(exp_s, k * (5 * NB) + (5 * n + 5))
                    dve.tensor_tensor(rden[:], rsum[:], sink_e[:], ALU.add).then_inc(soft_s, 1)
                    soft_done(n, 6)
                    dve.reciprocal(rden[:], rden[:]).then_inc(soft_s, 1)
                    soft_done(n, 7)
                    dve.tensor_tensor(prob[:, :, lo:], prob[:, :, lo:],
                                      rden[:].rearrange("p (g o) -> p g o", o=1).broadcast_to([P, G, 2 * P - lo]),
                                      ALU.mult).then_inc(soft_s, 1)

                def gate_attention(n):
                    def o_done(i):
                        if 3 * n + i:
                            dve.wait_ge(o_s, k * (3 * NB) + (3 * n + i))

                    dve.wait_ge(olo_s, k * NB + (n + 1))
                    o_done(0)
                    o_ps = ps[0:HD, OUT, :].rearrange("p (j e q) -> p e j q", j=2, e=2)
                    lo = o_lo[:].rearrange("p (j e q) -> p e j q", j=2, e=2)
                    for e in range(2):
                        dve.tensor_tensor(o_sum[e * HD:(e + 1) * HD], o_ps[:, e], lo[:, e], ALU.add).then_inc(o_s, 1)
                    o_done(2)
                    dve.wait_ge(ga_s, k * 4 + 4)
                    dve.scalar_tensor_tensor(out=tga[:, :, blk(n)], in0=tga[:, :, blk(n)], scalar=1.0,
                                             in1=o_sum[:], op0=ALU.add, op1=ALU.mult).then_inc(o_s, 1)

                for step, n in STEPS:
                    if step == "unit":
                        unit(n)
                    elif step == "scores":
                        softmax(n)
                        normalise(n)
                    elif step == "turn":
                        for kb in range(1 if n == 0 else 0, 2):
                            dve.wait_ge(pt_hi_s, k * NTURN + (turned(n, kb) + 1))
                            dve.tensor_tensor(pt_lo[:, kb], ps[:, TURN + kb, :], fp(pt_hi[:, kb]),
                                              ALU.subtract).then_inc(pt_lo_s, 1)
                    else:
                        gate_attention(n)
                soft_done(NB - 1, SOFT)
                conv_done(1, 12)
                dve.wait_ge(o_s, k * (3 * NB) + 3 * NB)
                dve.wait_ge(merge_s, k * 2 + 2)

            def mixer_low(h, m):
                dve.wait_ge(m_hi_s, DT * h + m + 1)
                dve.scalar_tensor_tensor(out=m_lo[h][:, m], in0=res[:, m, half(h)], scalar=0.5,
                                         in1=fp(m_hi[h][:, m]), op0=ALU.mult, op1=ALU.subtract).then_inc(m_lo_s, 1)

            def x_sum(h, m):
                dve.wait_ge(m_lo_s, DT * h + m + 1)
                dve.tensor_tensor(res[:, m, half(h)], fp(act_hi[:, m, half(h)]), fp(act_lo[:, m, half(h)]),
                                  ALU.add).then_inc(xsum_s, 1)

            def centre(q):
                dve.wait_ge(stat_s, 2 * q + 1)
                for m in range(DT):
                    tile = res[:, m, half(q % 2)]
                    dve.tensor_tensor(tile, tile, ps[:, stat_bank(q, 0), :], ALU.subtract).then_inc(cen_s, 1)

            def invert(q):
                dve.wait_ge(std_s, q + 1)
                dve.reciprocal(rstd[:], rstd[:]).then_inc(rstd_s, 1)
                dve.wait_ge(rstd_s, q + 1)

            def normalise_rows(q, ms):
                for m in ms:
                    tile = res[:, m, half(q % 2)]
                    dve.wait_ge(sq_s, 8 * q + m + 1)
                    dve.tensor_tensor(tile, tile, rstd[:], ALU.mult).then_inc(norm_s, 1)

            def norm_low(q, ms):
                for m in ms:
                    dve.wait_ge(n_hi_s, 8 * q + m + 1)
                    dve.tensor_tensor(act_lo[:, m, half(q)], res[:, m, half(q)], fp(act_hi[:, m, half(q)]),
                                      ALU.subtract).then_inc(n_lo_s, 1)

            def scale_residual(q):
                dve.wait_ge(n_lo_s, 8 * q + 8)
                for m in range(DT):
                    dve.tensor_scalar(res[:, m, half(q)], res[:, m, half(q)], ALPHA, None,
                                      ALU.mult).then_inc(scaled_s, 1)

            for m in range(DT):
                mixer_low(0, m)
            dve.memset(acc[:], 0.0).then_inc(res_s, 2)
            for v in range(OUT_TILES):
                h, m = v // DT, v % DT
                if h == 0:
                    x_sum(0, m)
                dve.wait_ge(out_s, v + 1)
                dve.wait_ge(xsum_s, DT * 2 if h else 2 * m + 1)
                dve.scalar_tensor_tensor(out=res[:, m, half(h)], in0=res[:, m, half(h)], scalar=ALPHA,
                                         in1=ps[:, v % 2, :], op0=ALU.mult, op1=ALU.add).then_inc(res_s, 1)
                if h == 0:
                    mixer_low(1, m)
                    x_sum(1, m)
                if v == DT:
                    dve.wait_ge(res_s, 2 + DT)
                    centre(0)
                if v == 11:
                    invert(0)
                    normalise_rows(0, range(4))
                if v == 12:
                    normalise_rows(0, range(4, DT))
                if v == 13:
                    norm_low(0, range(4))
                if v == 14:
                    norm_low(0, range(4, DT))
                if v == 15:
                    scale_residual(0)

            def hidden(g, h, t):
                dve.wait_ge(silu_s, g * 8 + (4 * h + 2 * t + 1))
                if h:
                    dve.wait_ge(hid_s, g * 12 + (3 * t + 3))
                dve.scalar_tensor_tensor(out=hid[:, t], in0=tanh_g[:, t], scalar=1.0, in1=ps[:, 2 * t, :],
                                         op0=ALU.add, op1=ALU.mult).then_inc(hid_s, 1)
                dve.wait_ge(f_s, g * 8 + (4 * h + 2 * t + 2))
                dve.wait_ge(hid_s, g * 12 + (6 * h + 3 * t + 1))
                dve.tensor_tensor(hid[:, t], hid[:, t], ps[:, 2 * t + 1, :], ALU.mult).then_inc(hid_s, 1)
                dve.wait_ge(silu_s, g * 8 + (4 * h + 2 * t + 2))
                dve.scalar_tensor_tensor(out=hid_lo[:, t, half(h)], in0=hid[:, t], scalar=0.5,
                                         in1=fp(hid_hi[:, t, half(h)]), op0=ALU.mult,
                                         op1=ALU.subtract).then_inc(hid_s, 1)

            dve.wait_ge(res_s, 2 + OUT_TILES)
            centre(1)
            hidden(0, 0, 0)
            invert(1)
            normalise_rows(1, range(DT))
            norm_low(1, range(DT))
            hidden(0, 0, 1)
            scale_residual(1)
            dve.wait_ge(scaled_s, 2 * DT)

            def add_down(g, v):
                h, m = v // DT, v % DT
                dve.wait_ge(d_s, g * 16 + (v + 1))
                dve.tensor_tensor(res[:, m, half(h)], res[:, m, half(h)], ps[:, 4 + v % 4, :],
                                  ALU.add).then_inc(add_s, 1)

            with dve.Fori(0, NG - 1) as g:
                hidden(g, 1, 0)
                hidden(g, 1, 1)
                for v in range(2 * DT):
                    add_down(g, v)
                dve.wait_ge(add_s, g * 16 + 16)
                dve.wait_ge(hid_s, g * 12 + 12)
                hidden(g + 1, 0, 0)
                hidden(g + 1, 0, 1)
            hidden(NG - 1, 1, 0)
            hidden(NG - 1, 1, 1)
            for v in range(2 * DT):
                add_down(NG - 1, v)
                if v == 11:
                    centre(2)
            invert(2)
            centre(3)
            normalise_rows(2, range(DT))
            invert(3)
            normalise_rows(3, range(DT))
            for i in range(NB):
                dve.wait_ge(ot_s, 2 * i + 2)
                if i >= 2:
                    dve.wait_ge(stored[i % 2], 16 * (i // 2))
                dve.tensor_copy(ost[:, i % 2, HALF:D], ps[:, 3 + 2 * (i % 3), :]).then_inc(ocp_dve, 1)

        @block.tensor
        def _(pe):
            def product(bank, w_h, w_l, a_hi, a_lo, tiles, ready=None):
                for t in range(tiles):
                    if ready is not None:
                        ready(t)
                    pe.matmul(bank, w_h(t), a_hi(t), start=(t == 0), stop=False)
                    pe.matmul(bank, w_h(t), a_lo(t), start=False, stop=False)
                    last = pe.matmul(bank, w_l(t), a_hi(t), start=False, stop=(t == tiles - 1))
                return last

            def project(slot, h, bank, ready=None):
                return product(ps[:, bank, :], lambda t: w_hi[:, slot, t], lambda t: w_lo[:, slot, t],
                               lambda t: act_hi[:, t, half(h)], lambda t: act_lo[:, t, half(h)], DT, ready)

            pe.wait_ge(tables, 2)

            def turn_x(i):
                st, cg = i // 2, i % 2
                pe.wait_ge(x_in[st], 16)
                if i >= 4:
                    pe.wait_ge(x_lo_s, i - 3)
                for c in range(4):
                    last = pe.transpose(ps[:, 4 + i % 4, blk(c)], xs[:, st, blk(4 * cg + c)], ident[:])
                last.then_inc(x_turned, 1)

            def turn_v(i):
                pe.wait_ge(v_copied, i + 1)
                if i >= 2:
                    pe.wait_ge(v_kept, 2 * (i - 1))
                for b in range(4):
                    last = pe.transpose(ps[:, 3 + i % 2, blk(b)], yc[:, (i % 2) * HALF + b * P:(i % 2) * HALF + (b + 1) * P],
                                        ident[:])
                last.then_inc(v_turned, 1)

            for i in range(8):
                turn_x(i)
            for n in range(2 * PRO_TILES):
                t, h = n // 2, n % 2
                if n == 1:
                    for i in range(8, 16):
                        turn_x(i)
                pe.wait_ge(w_lo_s, t + 1)
                pe.wait_ge(x_lo_s, 16 if h else 8)
                if n >= 3:
                    if n - 3 < 4:
                        pe.wait_ge(k_copied, 4 * (n - 2))
                    else:
                        pe.wait_ge(v_copied, n - 6)
                project(t % 2, h, unit_bank(n + 1)).then_inc(unit_s, 1)
                if n >= 5:
                    turn_v(n - 5)
            turn_v(3)

            pe.wait_ge(v_kept, 8)
            with pe.Fori(0, NKV) as k:
                for step, n in STEPS:
                    if step == "unit":
                        if n % 2 == 0:
                            pe.wait_ge(w_lo_s, k * NT + (PRO_TILES + n // 2 + 1))
                        if n == 2:
                            pe.wait_ge(q_hi_s, k * 8 + 2)
                        if n >= 3:
                            pe.wait_ge(*consumed(k, n - 3))
                        project((n // 2) % 2, n % 2, unit_bank(n)).then_inc(unit_s, 1)
                    elif step == "scores":
                        if n == 0:
                            pe.wait_ge(prep_dve, k * 9 + 2)
                            pe.wait_ge(q_lo_s, k * 8 + 8)
                        else:
                            pe.wait_ge(soft_s, k * (SOFT * NB) + (SOFT * (n - 1) + 1))
                        keys = slice(max(n - 1, 0) * P, (n + 1) * P)
                        for g in range(G):
                            dst = scores_ps[:, g, (P if n == 0 else 0):]
                            pe.matmul(dst, q_st[:, g, blk(n)], ks_hi[:, keys], start=True, stop=False)
                            last = pe.matmul(dst, q_st[:, g, blk(n)], ks_lo[:, keys], start=False, stop=True)
                        last.then_inc(scores_s, 1)
                    elif step == "turn":
                        pe.wait_ge(soft_s, k * (SOFT * NB) + (SOFT * n + SOFT))
                        if n:
                            pe.wait_ge(pt_lo_s, k * NTURN + turned(n, 0))
                        for kb in range(1 if n == 0 else 0, 2):
                            for g in range(G):
                                last = pe.transpose(ps[:, TURN + kb, blk(g)], prob[:, g, blk(kb)], ident[:])
                            last.then_inc(turn_s, 1)
                    else:
                        pe.wait_ge(pt_lo_s, k * NTURN + (turned(n, 1) + 1))
                        if n:
                            pe.wait_ge(o_s, k * (3 * NB) + (3 * (n - 1) + 2))
                        kbs = [1] if n == 0 else [0, 1]
                        for kb in kbs:
                            for part in (pt_hi, pt_lo):
                                last = pe.matmul(ps[:, OUT, :], vs[:, n - 1 + kb, :], part[:, kb],
                                                 start=(kb == kbs[0] and part is pt_hi),
                                                 stop=(kb == 1 and part is pt_lo))
                        last.then_inc(values_s, 1)
                pe.wait_ge(conv_s, k * 24 + 22)
                pe.wait_ge(gc_s, k * 4 + 3)
                pe.wait_ge(o_s, k * (3 * NB) + (3 * NB - 1))

            def stat(q, which):
                if which == 0:
                    pe.wait_ge(acc_s, 7 * (q + 1))
                else:
                    pe.wait_ge(sqacc_s, 7 * (q + 1))
                pe.matmul(ps[:, stat_bank(q, which), :], mean_of[:], (acc2 if which else acc)[:],
                          start=True, stop=True).then_inc(stat_s, 1)

            def project_out(h, v, slot, bank):
                pe.wait_ge(w_lo_s, v + (IN_TILES + 1))
                pe.wait_ge(res_s, v + 1)
                return product(ps[:, bank, :], lambda t: w_hi[:, slot, t], lambda t: w_lo[:, slot, t],
                               lambda t: m_hi[h][:, t], lambda t: m_lo[h][:, t], DT,
                               lambda t: pe.wait_ge(m_lo_s, DT * h + t + 1)).then_inc(out_s, 1)

            with pe.Fori(0, DT // 2) as i:
                for e in range(2):
                    project_out(0, i * 2 + e, e, e)
            for v in range(DT, 2 * DT):
                project_out(1, v, v % 2, v % 2)
                if v == DT:
                    stat(0, 0)
                if v == DT + 3:
                    stat(0, 1)

            def gate_up(g, h, s, ready=None):
                if h == 0:
                    pe.wait_ge(fw_lo_s, g * 6 + (s + 1))
                w_h, w_l = ffn_hi(s), ffn_lo(s)
                product(ps[:, s, :], lambda t: w_h[:, t], lambda t: w_l[:, t],
                        lambda t: act_hi[:, t, half(h)], lambda t: act_lo[:, t, half(h)], DT,
                        ready).then_inc(f_s, 1)

            def down(g, h, m):
                v = h * DT + m
                if m == 0:
                    pe.wait_ge(fw_lo_s, g * 6 + 6)
                    pe.wait_ge(hid_s, g * 12 + 6 * (h + 1))
                if v >= 4:
                    pe.wait_ge(add_s, g * 16 + (v - 3))
                product(ps[:, 4 + v % 4, :], lambda t: wd_hi[:, t, blk(m)], lambda t: wd_lo[:, t, blk(m)],
                        lambda t: hid_hi[:, t, half(h)], lambda t: hid_lo[:, t, half(h)], 2).then_inc(d_s, 1)

            pe.wait_ge(n_lo_s, DT)
            pe.wait_ge(res_s, 2 + OUT_TILES)
            gate_up(0, 0, 0)
            stat(1, 0)
            gate_up(0, 0, 1)
            gate_up(0, 0, 2)
            stat(1, 1)
            gate_up(0, 0, 3)

            def second_half(g):
                for s in range(4):
                    pe.wait_ge(hid_s, g * 12 + (3 * (s // 2) + 1 + s % 2))
                    gate_up(g, 1, s, (lambda t: pe.wait_ge(n_lo_s, DT + t + 1)) if s == 0 else None)

            with pe.Fori(0, NG - 1) as g:
                second_half(g)
                for h in range(2):
                    for m in range(DT):
                        down(g, h, m)
                for s in range(4):
                    pe.wait_ge(hid_s, g * 12 + (6 + 3 * (s // 2) + 1 + s % 2))
                    gate_up(g + 1, 0, s)
                pe.wait_ge(add_s, g * 16 + 2 * DT)
            second_half(NG - 1)
            for m in range(DT):
                down(NG - 1, 0, m)
            for m in range(DT):
                down(NG - 1, 1, m)
                if m == 3:
                    stat(2, 0)
            stat(2, 1)
            stat(3, 0)
            stat(3, 1)
            for i in range(NB):
                pe.wait_ge(aff_s, 8 * (2 + i // 4) + 8)
                if i >= 3:
                    pe.wait_ge(ocp_act, i - 2)
                    pe.wait_ge(ocp_dve, i - 2)
                for c in range(DT):
                    last = pe.transpose(ps[:, 2 + 2 * (i % 3) + c // 4, blk(c % 4)], res[:, c, blk(i)], ident[:])
                    if c % 4 == 3:
                        last.then_inc(ot_s, 1)


_INS = ["x", "w_in", "conv_w", "attn_sinks", "w_out", "ln1_g", "ln1_b", "w_gate", "w_up", "w_down", "ln2_g", "ln2_b"]


def kernel(**inputs):
    import concourse.bacc as bacc
    from concourse.bass_utils import run_bass_kernel_spmd

    nc = bacc.Bacc("TRN2", target_bir_lowering=False, num_devices=1)
    arrays, args = {}, []
    for name in _INS:
        a = np.ascontiguousarray(inputs[name])
        arrays[f"in_{name}"] = a
        args.append(nc.dram_tensor(f"in_{name}", a.shape, mybir.dt.from_np(a.dtype), kind="ExternalInput").ap())
    out = nc.dram_tensor("out", (1, S, D), F32, kind="ExternalOutput").ap()
    build(nc, *args, out)
    r = run_bass_kernel_spmd(nc, [arrays], core_ids=[0])
    return r.results[0]["out"]
```

```python
from contextlib import ExitStack

import numpy as np

import concourse.bass as bass
from concourse import mybir

F32 = mybir.dt.float32
F32R = mybir.dt.float32r
ALU = mybir.AluOpType
ACT = mybir.ActivationFunctionType
AX_X = mybir.AxisListType.X

P = 128
D = 1024
S = 1024
DT = D // P
HALF = 512
HD = 64
NQ, NKV = 16, 4
G = NQ // NKV
NB = S // P
DFF = 2816
FT = DFF // P
NG = FT // 2
ALPHA = 2.0 ** 0.25
EPS = 1e-5
NEG = -1e30
SCALE = HD ** -0.5

COL_Q, COL_K, COL_V = 0, D, D + NKV * HD
COL_CB = COL_V + NKV * HD
COL_CC, COL_CH, COL_GC, COL_GA = (COL_CB + D * n for n in (1, 2, 3, 4))

PRO_TILES = 4
TILES = [("q", 0), ("q", 1), ("ga", 0), ("ga", 1)] + [(x, j) for j in (0, 1) for x in ("cc", "ch", "cb", "gc")]
NT = len(TILES)
IN_TILES = PRO_TILES + NKV * NT
OUT_TILES = 2 * DT
COLS = {"q": COL_Q, "ga": COL_GA, "cc": COL_CC, "ch": COL_CH, "cb": COL_CB, "gc": COL_GC}


def head_schedule():
    first = 4
    steps = []
    for u in range(2 * NT):
        v = u - first
        if v >= 2 and v % 2 == 0 and (v - 2) // 2 < NB:
            steps.append(("scores", (v - 2) // 2))
        steps.append(("unit", u))
        if v >= 3 and v % 2 == 1 and (v - 3) // 2 < NB:
            steps.append(("turn", (v - 3) // 2))
        if v >= 4 and v % 2 == 0 and (v - 4) // 2 < NB:
            steps.append(("values", (v - 4) // 2))
    return steps


STEPS = head_schedule()

SOFT = 8


def turned(n, kb):
    return 0 if n == 0 else 2 * n - 1 + kb


NTURN = 2 * NB - 1


def build(nc, x, w_in, conv_w, sinks, w_out, ln1_g, ln1_b, w_gate, w_up, w_down, ln2_g, ln2_b, out):
    ctx = ExitStack()
    with ctx:
        def sem(name):
            return ctx.enter_context(nc.semaphore(name))

        def sb(stack, name, shape, dt=F32):
            return stack.enter_context(nc.sbuf_tensor(name, shape, dt))

        act_hi = sb(ctx, "act_hi", [P, DT, S], F32R)
        act_lo = sb(ctx, "act_lo", [P, DT, S], F32R)
        res = sb(ctx, "res", [P, DT, S])
        raw = sb(ctx, "raw", [P, 2, DT, P])
        w_hi = sb(ctx, "w_hi", [P, 2, DT, P], F32R)
        w_lo = sb(ctx, "w_lo", [P, 2, DT, P], F32R)
        ident = sb(ctx, "ident", [P, P])
        mean_of = sb(ctx, "mean_of", [P, P])
        cw = sb(ctx, "cw", [P, DT, 3])
        snk = sb(ctx, "snk", [P, NQ])
        lng = sb(ctx, "lng", [P, DT])
        lnb = sb(ctx, "lnb", [P, DT])
        std = sb(ctx, "std", [P, NB // 2])
        inv = sb(ctx, "inv", [P, NB // 2])
        eps = sb(ctx, "eps", [P, 1])

        with ExitStack() as st:
            q_st = sb(st, "q_st", [P, G, S], F32R)
            pt_hi = sb(st, "pt_hi", [P, 2, G * P], F32R)
            pt_lo = sb(st, "pt_lo", [P, 2, G * P], F32R)
            prob = sb(st, "prob", [P, G, 2 * P])
            tga = sb(st, "tga", [P, 2, S])
            ks_hi = sb(st, "ks_hi", [P, S], F32R)
            ks_lo = sb(st, "ks_lo", [P, S], F32R)
            vs = sb(st, "vs", [P, NB, 2 * HD], F32R)
            bias = sb(st, "bias", [P, G, 2 * P])
            negdist = sb(st, "negdist", [P, 2 * P])
            mask = sb(st, "mask", [P, 2 * P])
            slope = sb(st, "slope", [P, G])
            snkc = sb(st, "snkc", [P, G])
            cwc = sb(st, "cwc", [P, 2, 3])
            ccs = sb(st, "ccs", [P, S])
            u_pad = sb(st, "u_pad", [P, 2 + S])
            yc = sb(st, "yc", [P, S])
            tgc = sb(st, "tgc", [P, S])
            o_lo = sb(st, "o_lo", [HD, G * P])
            o_sum = sb(st, "o_sum", [P, 2, P])
            mx = sb(st, "mx", [P, G])
            neg_m = sb(st, "neg_m", [P, G])
            sink_d = sb(st, "sink_d", [P, G])
            sink_e = sb(st, "sink_e", [P, G])
            rsum = sb(st, "rsum", [P, G])
            rden = sb(st, "rden", [P, G])
        with ExitStack() as st:
            xs = sb(st, "xs", [P, NB, D])

        late = ctx.enter_context(ExitStack())
        with ExitStack() as st:
            acc = sb(st, "acc", [P, HALF])
            sq_acc = sb(st, "sq_acc", [P, 2, HALF])
            sq = sb(st, "sq", [P, 2, HALF])
        ln2_rows = sb(late, "ln2_rows", [P, 2, D])
        sb(late, "spare", [P, HALF])
        raw_b = sb(late, "raw_b", [P, 2, DT, P])
        with ExitStack() as st:
            m_hi, m_lo = [], []
            for h in range(2):
                m_hi.append(sb(st, f"m_hi{h}", [P, DT, HALF], F32R))
                m_lo.append(sb(st, f"m_lo{h}", [P, DT, HALF], F32R))
        with ExitStack() as st:
            w_hi_b = sb(st, "w_hi_b", [P, 2, DT, P], F32R)
            w_lo_b = sb(st, "w_lo_b", [P, 2, DT, P], F32R)
            wd_hi = sb(st, "wd_hi", [P, 2, D], F32R)
            wd_lo = sb(st, "wd_lo", [P, 2, D], F32R)
            raw_d = sb(st, "raw_d", [P, 2, D])
            hid_hi = sb(st, "hid_hi", [P, 2, S], F32R)
            hid_lo = sb(st, "hid_lo", [P, 2, S], F32R)
            tanh_g = sb(st, "tanh_g", [P, 2, HALF])
            hid = sb(st, "hid", [P, 2, HALF])
        with ExitStack() as st:
            ost = sb(st, "ost", [P, 4, D])
            bn = sb(st, "bn", [P, 2, 2, 6])
            mv = sb(st, "mv", [P, 2, 2])
            neg_mean = sb(st, "neg_mean", [P, 2])
            std2 = sb(st, "std2", [P, 2])
            inv2 = sb(st, "inv2", [P, 2])

        ps = ctx.enter_context(nc.psum_tensor("ps", [P, 8, HALF], F32))
        SCORE, TURN, OUT = 3, 5, 7
        scores_ps = ps[:, SCORE:SCORE + 2, :].rearrange("p b (g k) -> p (b g) k", k=2 * P)

        x_in = [sem(f"x_in{i}") for i in range(NB)]
        params_in = sem("params_in")
        w_in_s = [sem(f"w_landed{i}") for i in range(2)]
        tables = sem("tables")
        x_turned, x_hi_s, x_lo_s = sem("x_turned"), sem("x_hi_done"), sem("x_lo_done")
        w_hi_s, w_lo_s = sem("w_hi_done"), sem("w_lo_done")
        unit_s = sem("unit_done")
        k_copied, v_copied, v_turned, v_kept = sem("k_copied"), sem("v_copied"), sem("v_turned"), sem("v_kept")
        prep_act, prep_dve = sem("head_prep_act"), sem("head_prep_dve")
        q_hi_s, q_lo_s = sem("q_hi_done"), sem("q_lo_done")
        ga_s, cc_s, gc_s = sem("ga_tanh_done"), sem("cc_copied"), sem("gc_tanh_done")
        conv_s = sem("conv_step")
        scores_s, soft_s, exp_s = sem("scores_done"), sem("softmax_step"), sem("exp_done")
        turn_s, pt_hi_s, pt_lo_s = sem("probs_turned"), sem("pt_hi_done"), sem("pt_lo_done")
        values_s, olo_s, o_s = sem("values_done"), sem("o_lo_copied"), sem("o_step")
        merge_s = sem("merge_done")
        m_hi_s, m_lo_s, xsum_s = sem("m_hi_done"), sem("m_lo_done"), sem("x_sum_done")
        out_s, res_s = sem("out_unit_done"), sem("res_tile_done")
        acc_s, cen_s, sq_s = sem("channel_sum_step"), sem("centred"), sem("squared")
        even_s, odd_s, stat_s = sem("even_squares_step"), sem("odd_squares_step"), sem("stat_done")
        std_s, inv_s, norm_s = sem("std_done"), sem("inverse_done"), sem("normalised")
        n_hi_s, n_lo_s, scaled_s = sem("norm_hi_done"), sem("norm_lo_done"), sem("residual_scaled")
        fw_in = [sem(f"ffn_w_landed{i}") for i in range(6)]
        fw_hi_s, fw_lo_s = sem("ffn_w_hi_done"), sem("ffn_w_lo_done")
        f_s, d_s = sem("gate_up_unit_done"), sem("down_unit_done")
        silu_s, hid_s, add_s = sem("silu_act_step"), sem("hidden_step"), sem("down_added")
        rows_in = sem("ln2_rows_in")
        ot_s, bn_s, std2_s, inv2_s = sem("rows_turned"), sem("row_stats_step"), sem("row_std_done"), sem("row_inverse_done")
        rcen_s, rgam_s, rout_s = sem("rows_centred"), sem("rows_scaled"), sem("rows_done")
        stored = [sem(f"stored{i}") for i in range(4)]

        block = ctx.enter_context(nc.Block())

        def half(h):
            return slice(h * HALF, (h + 1) * HALF)

        def blk(n):
            return slice(n * P, (n + 1) * P)

        def fp(ap):
            return ap.bitcast(F32)

        def unit_bank(u):
            return u % 3

        def consumed(k, u):
            kind, j = TILES[u // 2]
            h = u % 2
            if kind == "q":
                return q_lo_s, 8 * k + 4 * j + 2 * h + 2
            if kind == "ga":
                return ga_s, 4 * k + 2 * j + h + 1
            if kind == "cc":
                return cc_s, 4 * k + 2 * j + h + 1
            if kind == "gc":
                return gc_s, 4 * k + 2 * j + h + 1
            return conv_s, 24 * k + 12 * j + (4 * h + 1 if kind == "ch" else 9 + h)

        def ffn_raw(s):
            return raw_b[:, s] if s < 2 else raw[:, s - 2] if s < 4 else raw_d[:, s - 4]

        def ffn_hi(s):
            return w_hi_b[:, s] if s < 2 else w_hi[:, s - 2] if s < 4 else wd_hi[:, s - 4]

        def ffn_lo(s):
            return w_lo_b[:, s] if s < 2 else w_lo[:, s - 2] if s < 4 else wd_lo[:, s - 4]

        MEAN, VAR, INV = 6, 7, 5
        ROW_BANKS = [0, 2, 0, 2, 4, 6, 0, 2]

        def row_banks(i):
            return ps[:, ROW_BANKS[i]:ROW_BANKS[i] + 2, :]

        @block.sync
        def _(sp):
            def load_w(tile_slot, w, col):
                src = w[0, :, bass.ds(col, P)].rearrange("(t p) c -> p t c", p=P)
                sp.dma_start(raw[:, tile_slot], src).then_inc(w_in_s[tile_slot], 16)

            for i in range(4):
                sp.dma_start(xs[:, i, :], x[0, blk(i), :]).then_inc(x_in[i], 16)
            load_w(0, w_in, COL_K)
            for i in range(4, NB):
                sp.dma_start(xs[:, i, :], x[0, blk(i), :]).then_inc(x_in[i], 16)
            load_w(1, w_in, COL_K + P)
            with nc.allow_non_contiguous_dma(reason="per-channel parameters, loaded once"):
                sp.dma_start(snk[:], sinks[0:1, :].partition_broadcast(P)).then_inc(params_in, 16)
                for t in range(3):
                    sp.dma_start(cw[:, :, t], conv_w[0, t].rearrange("(m p) -> p m", p=P)).then_inc(params_in, 16)
                for dst, src in ((lng, ln1_g), (lnb, ln1_b)):
                    sp.dma_start(dst[:], src[0].rearrange("(m p) -> p m", p=P)).then_inc(params_in, 16)
            for t in (2, 3):
                sp.wait_ge(w_lo_s, t - 1)
                load_w(t % 2, w_in, COL_V + P * (t - 2))
            with sp.Fori(0, NKV) as k:
                for i, (kind, j) in enumerate(TILES):
                    sp.wait_ge(w_lo_s, k * NT + (PRO_TILES + i - 1))
                    load_w(i % 2, w_in, k * (2 * P) + (COLS[kind] + P * j))
            def load_ffn(g, s):
                if s < 4:
                    w = (w_gate, w_up)[s % 2]
                    src = w[0, :, bass.ds(g * (2 * P) + P * (s // 2), P)].rearrange("(t p) c -> p t c", p=P)
                else:
                    src = w_down[0, bass.ds(g * (2 * P) + P * (s - 4), P), :]
                sp.dma_start(ffn_raw(s), src).then_inc(fw_in[s], 16)

            for v in range(OUT_TILES):
                sp.wait_ge(w_lo_s, IN_TILES + v - 1)
                load_w(v % 2, w_out, P * (v % DT))
                if v == DT:
                    sp.wait_ge(merge_s, 2 * NKV)
                    load_ffn(0, 0)
                    load_ffn(0, 1)
            for s in (2, 3):
                sp.wait_ge(w_lo_s, IN_TILES + OUT_TILES - 3 + s)
                load_ffn(0, s)
            sp.wait_ge(out_s, OUT_TILES)
            load_ffn(0, 4)
            load_ffn(0, 5)
            with sp.Fori(1, NG) as g:
                for s in range(6):
                    sp.wait_ge(fw_lo_s, g * 6 + (s - 5))
                    load_ffn(g, s)
            sp.wait_ge(scaled_s, 2 * DT)
            for n, row in enumerate((ln2_g, ln2_b)):
                sp.dma_start(ln2_rows[:, n, :], row[0:1, :].partition_broadcast(P)).then_inc(rows_in, 16)
            for i in range(NB):
                sp.wait_ge(rout_s, i + 1)
                sp.dma_start(out[0, blk(i), :], ost[:, i % 4, :]).then_inc(stored[i % 4], 16)
            for i in range(4):
                sp.wait_ge(stored[i], 16 * NB // 4)

        @block.gpsimd
        def _(pool):
            pool.memset(ident[:], 0.0).then_inc(tables, 1)
            pool.wait_ge(tables, 1)
            pool.affine_select(out=ident[:], in_=ident[:], compare_op=ALU.not_equal, fill=1.0, base=0,
                               pattern=[[-1, P]], channel_multiplier=1).then_inc(tables, 1)
            pool.memset(mean_of[:], 1.0 / D).then_inc(tables, 1)
            pool.memset(eps[:], EPS).then_inc(tables, 1)
            pool.memset(u_pad[:, 0:2], 0.0).then_inc(tables, 1)
            pool.iota(negdist[:], pattern=[[1, 2 * P]], base=-P, channel_multiplier=-1,
                      allow_small_or_imprecise_dtypes=True).then_inc(tables, 1)
            pool.memset(mask[:], 0.0).then_inc(tables, 1)
            pool.wait_ge(tables, 7)
            pool.affine_select(out=mask[:], in_=mask[:], compare_op=ALU.is_ge, fill=NEG, base=P,
                               pattern=[[-1, 2 * P]], channel_multiplier=1).then_inc(tables, 1)
            pool.wait_ge(tables, 8)
            pool.affine_select(out=mask[:], in_=mask[:], compare_op=ALU.is_ge, fill=NEG, base=-1,
                               pattern=[[1, 2 * P]], channel_multiplier=-1).then_inc(tables, 1)
            for g in range(G):
                pool.memset(slope[:, g:g + 1], float(np.float32(2.0 ** (-8.0 * (g + 1) / NQ)))).then_inc(tables, 1)

            def low_part(count, slot):
                pool.wait_ge(w_hi_s, count)
                pool.tensor_tensor(w_lo[:, slot], raw[:, slot], fp(w_hi[:, slot]), ALU.subtract).then_inc(w_lo_s, 1)

            for t in range(6):
                low_part(t + 1, t % 2)
            with pool.Fori(0, NKV) as k:
                for i in range(NT):
                    low_part(k * NT + (6 + i + 1), i % 2)

            def ffn_low_part(g, s):
                pool.wait_ge(fw_hi_s, g * 6 + (s + 1))
                pool.tensor_tensor(ffn_lo(s), ffn_raw(s), fp(ffn_hi(s)), ALU.subtract).then_inc(fw_lo_s, 1)

            def channel_sum(q, m):
                if m == 0:
                    return
                pool.wait_ge(res_s, 2 + DT * q + m + 1)
                first = res[:, 0, half(q)] if m == 1 else acc[:]
                if m == 1:
                    if q:
                        pool.wait_ge(stat_s, 1)
                else:
                    pool.wait_ge(acc_s, 7 * q + m - 1)
                pool.tensor_tensor(acc[:], first, res[:, m, half(q)], ALU.add).then_inc(acc_s, 1)

            def even_squares(q):
                for m in (2, 4, 6):
                    pool.wait_ge(sq_s, 8 * q + m + 1)
                    if m > 2:
                        pool.wait_ge(even_s, 3 * q + m // 2 - 1)
                    pool.tensor_tensor(sq_acc[:, 0], sq_acc[:, 0], sq[:, 0], ALU.add).then_inc(even_s, 1)

            for v in range(OUT_TILES):
                if v + 2 < OUT_TILES:
                    low_part(IN_TILES + v + 3, v % 2)
                if v in (11, 12):
                    ffn_low_part(0, v - 11)
                channel_sum(v // DT, v % DT)
                if v == DT:
                    even_squares(0)
            ffn_low_part(0, 2)
            ffn_low_part(0, 3)
            even_squares(1)
            ffn_low_part(0, 4)
            ffn_low_part(0, 5)
            with pool.Fori(1, NG) as g:
                for s in range(6):
                    ffn_low_part(g, s)
            pool.wait_ge(rows_in, 32)
            for i in range(NB):
                pool.wait_ge(rgam_s, i + 1)
                pool.tensor_tensor(ost[:, i % 4, :], ost[:, i % 4, :], ln2_rows[:, 1, :], ALU.add).then_inc(rout_s, 1)

        @block.scalar
        def _(act):
            def high_part(landed, slot, free, count):
                act.wait_ge(w_in_s[slot], landed)
                if free is not None:
                    act.wait_ge(free, count)
                act.activation(w_hi[:, slot], raw[:, slot], ACT.Copy).then_inc(w_hi_s, 1)

            def x_high(i):
                act.wait_ge(x_turned, i + 1)
                st, cg = i // 2, i % 2
                act.activation(act_hi[:, 4 * cg:4 * cg + 4, blk(st)],
                               ps[:, 4 + i % 4, :].rearrange("p (c s) -> p c s", c=4), ACT.Copy).then_inc(x_hi_s, 1)

            for i in range(8):
                x_high(i)
            high_part(16, 0, None, 0)
            for i in range(8, 16):
                x_high(i)
            high_part(16, 1, None, 0)
            for n in range(2 * PRO_TILES):
                t, h = n // 2, n % 2
                act.wait_ge(unit_s, n + 1)
                bank = ps[:, unit_bank(n + 1), :]
                if t < 2:
                    act.wait_ge(x_lo_s, 16)
                    for e in range(2):
                        for to in range(2):
                            act.activation(res[to * HD:(to + 1) * HD, 2 * (2 * t + e), half(h)],
                                           bank[e * HD:(e + 1) * HD, :], ACT.Copy).then_inc(k_copied, 1)
                else:
                    i = n - 4
                    if i >= 2:
                        act.wait_ge(v_turned, i - 1)
                    act.activation(yc[:, half(i % 2)], bank, ACT.Copy).then_inc(v_copied, 1)
                if h == 1:
                    high_part(16 * ((t + 2) // 2 + 1), t % 2, unit_s, n + 1)

            act.wait_ge(v_kept, 8)
            with act.Fori(0, NKV) as k:
                act.activation(ks_hi[:], res[:, bass.ds(k * 2, 1), :].rearrange("p a s -> p (a s)"), ACT.Copy).then_inc(prep_act, 1)
                act.activation(vs[:, :, 0:HD],
                               res[:, bass.ds(k * 2 + 1, 1), 0:NB * HD].rearrange("p a (b d) -> p (a b) d", b=NB),
                               ACT.Copy).then_inc(prep_act, 1)
                for step, n in STEPS:
                    if step == "unit":
                        kind, j = TILES[n // 2]
                        h = n % 2
                        bank = ps[:, unit_bank(n), :]
                        done = k * (2 * NT) + (2 * PRO_TILES + n + 1)
                        if kind in ("q", "ga", "cc", "gc"):
                            act.wait_ge(unit_s, done)
                        if kind == "q":
                            for e in range(2):
                                rows = slice(e * HD, (e + 1) * HD)
                                act.activation(q_st[rows, 2 * j + e, half(h)], bank[rows, :],
                                               ACT.Copy).then_inc(q_hi_s, 1)
                        elif kind == "ga":
                            act.activation(tga[:, j, half(h)], bank, ACT.Tanh, scale=0.5).then_inc(ga_s, 1)
                        elif kind == "cc":
                            if j:
                                act.wait_ge(conv_s, k * 24 + 12)
                            act.activation(ccs[:, half(h)], bank, ACT.Copy).then_inc(cc_s, 1)
                        elif kind == "gc":
                            if j:
                                act.wait_ge(conv_s, k * 24 + 12)
                            act.activation(tgc[:, half(h)], bank, ACT.Tanh, scale=0.5).then_inc(gc_s, 1)
                        if h == 1:
                            i = n // 2
                            high_part(k * (16 * NT // 2) + 16 * ((PRO_TILES + i + 2) // 2 + 1), i % 2, unit_s, done)
                    elif step == "scores":
                        lo = P if n == 0 else 0
                        act.wait_ge(soft_s, k * (SOFT * NB) + (SOFT * n + 5))
                        act.activation(sink_e[:], sink_d[:], ACT.Exp).then_inc(exp_s, 1)
                        for g in range(G):
                            act.activation(prob[:, g, lo:], prob[:, g, lo:], ACT.Exp, bias=neg_m[:, g:g + 1],
                                           accum_out=rsum[:, g:g + 1]).then_inc(exp_s, 1)
                    elif step == "turn":
                        for kb in range(1 if n == 0 else 0, 2):
                            i = k * NTURN + (turned(n, kb) + 1)
                            act.wait_ge(turn_s, i)
                            act.activation(pt_hi[:, kb], ps[:, TURN + kb, :], ACT.Copy).then_inc(pt_hi_s, 1)
                    else:
                        act.wait_ge(values_s, k * NB + (n + 1))
                        if n:
                            act.wait_ge(o_s, k * (3 * NB) + 3 * n)
                        act.activation(o_lo[:], ps[HD:P, OUT, :], ACT.Copy).then_inc(olo_s, 1)
                act.wait_ge(merge_s, k * 2 + 2)

            for h in range(2):
                for m in range(DT):
                    act.activation(m_hi[h][:, m], res[:, m, half(h)], ACT.Copy, scale=0.5).then_inc(m_hi_s, 1)

            def ffn_high_part(g, s, free, count):
                act.wait_ge(fw_in[s], (g + 1) * 16)
                act.wait_ge(free, count)
                act.activation(ffn_hi(s), ffn_raw(s), ACT.Copy).then_inc(fw_hi_s, 1)

            def squares(q):
                for m in range(DT):
                    act.wait_ge(cen_s, 8 * q + m + 1)
                    if m >= 2 and 3 * q + (m - 2) // 2:
                        act.wait_ge((even_s, odd_s)[m % 2], 3 * q + (m - 2) // 2)
                    dst = sq_acc[:, m] if m < 2 else sq[:, m % 2]
                    act.activation(dst, res[:, m, half(q)], ACT.Square).then_inc(sq_s, 1)

            def root(q):
                act.wait_ge(stat_s, 3 * q + 2)
                act.activation(std[:], ps[:, VAR, 0:4], ACT.Sqrt, bias=eps[:]).then_inc(std_s, 1)

            def norm_high(q, ms):
                for m in ms:
                    act.wait_ge(norm_s, 8 * q + m + 1)
                    act.activation(act_hi[:, m, half(q)], res[:, m, half(q)], ACT.Identity,
                                   bias=lnb[:, m:m + 1]).then_inc(n_hi_s, 1)

            act.wait_ge(params_in, 16 * 6)
            for v in range(OUT_TILES):
                if v + 2 < OUT_TILES:
                    t = IN_TILES + v + 2
                    high_part(16 * (t // 2 + 1), v % 2, out_s, v + 1)
                if v in (11, 12):
                    ffn_high_part(0, v - 11, out_s, DT)
                if v == DT:
                    squares(0)
                if v == DT + 1:
                    root(0)
                    norm_high(0, range(4))
                if v == DT + 2:
                    norm_high(0, range(4, DT))
            ffn_high_part(0, 2, out_s, OUT_TILES - 1)
            ffn_high_part(0, 3, out_s, OUT_TILES)

            def silu(g, h, t):
                act.wait_ge(f_s, g * 8 + (4 * h + 2 * t + 1))
                if h:
                    act.wait_ge(hid_s, g * 12 + (3 * t + 1))
                act.activation(tanh_g[:, t], ps[:, 2 * t, :], ACT.Tanh, scale=0.5).then_inc(silu_s, 1)
                act.wait_ge(hid_s, g * 12 + (6 * h + 3 * t + 2))
                act.activation(hid_hi[:, t, half(h)], hid[:, t], ACT.Copy, scale=0.5).then_inc(silu_s, 1)

            squares(1)
            silu(0, 0, 0)
            root(1)
            norm_high(1, range(DT))
            silu(0, 0, 1)
            ffn_high_part(0, 4, out_s, OUT_TILES)
            ffn_high_part(0, 5, out_s, OUT_TILES)

            with act.Fori(0, NG - 1) as g:
                silu(g, 1, 0)
                silu(g, 1, 1)
                for s in range(4):
                    ffn_high_part(g + 1, s, f_s, g * 8 + 8)
                for s in (4, 5):
                    ffn_high_part(g + 1, s, d_s, g * 16 + 16)
                act.wait_ge(hid_s, g * 12 + 12)
                silu(g + 1, 0, 0)
                silu(g + 1, 0, 1)
            silu(NG - 1, 1, 0)
            silu(NG - 1, 1, 1)
            def row_centre(i):
                act.wait_ge(bn_s, 4 * i + 3)
                act.activation(std2[:, i % 2:i % 2 + 1], mv[:, i % 2, 1:2], ACT.Sqrt, bias=eps[:]).then_inc(std2_s, 1)
                act.wait_ge(bn_s, 4 * i + 4)
                if i >= 4:
                    act.wait_ge(stored[i % 4], 16 * (i // 4))
                act.activation(ost[:, i % 4, :].rearrange("p (b s) -> p b s", b=2), row_banks(i), ACT.Identity,
                               bias=neg_mean[:, i % 2:i % 2 + 1]).then_inc(rcen_s, 1)

            for i in range(NB):
                row_centre(i)

        @block.vector
        def _(dve):
            dve.wait_ge(tables, 13)
            for i in range(16):
                dve.wait_ge(x_hi_s, i + 1)
                st, cg = i // 2, i % 2
                dst = (slice(None), slice(4 * cg, 4 * cg + 4), blk(st))
                dve.tensor_tensor(act_lo[dst], ps[:, 4 + i % 4, :].rearrange("p (c s) -> p c s", c=4),
                                  fp(act_hi[dst]), ALU.subtract).then_inc(x_lo_s, 1)
            for i in range(4):
                j, h = i // 2, i % 2
                dve.wait_ge(v_turned, i + 1)
                src = ps[:, 3 + i % 2, :].rearrange("p (b e d) -> p e b d", b=4, e=2)
                for e in range(2):
                    dst = res[:, 2 * (2 * j + e) + 1, 4 * HD * h:4 * HD * (h + 1)].rearrange("p (b d) -> p b d", b=4)
                    dve.tensor_copy(dst, src[:, e]).then_inc(v_kept, 1)
            dve.wait_ge(params_in, 16 * 6)

            with dve.Fori(0, NKV) as k:
                def prep_done(n):
                    dve.wait_ge(prep_dve, k * 9 + n)

                dve.wait_ge(prep_act, k * 2 + 1)
                dve.tensor_tensor(ks_lo[:], res[:, bass.ds(k * 2, 1), :].rearrange("p a s -> p (a s)"),
                                  fp(ks_hi[:]), ALU.subtract).then_inc(prep_dve, 1)
                dve.wait_ge(prep_act, k * 2 + 2)
                dve.tensor_tensor(vs[:, :, HD:2 * HD],
                                  res[:, bass.ds(k * 2 + 1, 1), 0:NB * HD].rearrange("p a (b d) -> p (a b) d", b=NB),
                                  fp(vs[:, :, 0:HD]), ALU.subtract).then_inc(prep_dve, 1)
                for g in range(G):
                    dve.scalar_tensor_tensor(out=bias[:, g], in0=negdist[:], scalar=slope[:, g:g + 1], in1=mask[:],
                                             op0=ALU.mult, op1=ALU.add).then_inc(prep_dve, 1)
                prep_done(6)
                dve.tensor_scalar(slope[:], slope[:], 2.0 ** (-8.0 * G / NQ), None, ALU.mult).then_inc(prep_dve, 1)
                dve.tensor_copy(snkc[:], snk[:, bass.ds(k * G, G)]).then_inc(prep_dve, 1)
                dve.tensor_copy(cwc[:], cw[:, bass.ds(k * 2, 2), :]).then_inc(prep_dve, 1)
                prep_done(9)

                def conv_done(j, n):
                    if 12 * j + n:
                        dve.wait_ge(conv_s, k * 24 + (12 * j + n))

                def unit(n):
                    kind, j = TILES[n // 2]
                    h = n % 2
                    bank = ps[:, unit_bank(n), :]
                    done = k * (2 * NT) + (2 * PRO_TILES + n + 1)
                    cols = half(h)
                    if kind == "q":
                        for e in range(2):
                            rows, other = slice(e * HD, (e + 1) * HD), slice((1 - e) * HD, (2 - e) * HD)
                            dve.wait_ge(q_hi_s, k * 8 + (4 * j + 2 * h + 2))
                            dve.tensor_tensor(q_st[other, 2 * j + e, cols], bank[rows, :],
                                              fp(q_st[rows, 2 * j + e, cols]), ALU.subtract).then_inc(q_lo_s, 1)
                    elif kind == "ch":
                        dve.wait_ge(unit_s, done)
                        dve.wait_ge(cc_s, k * 4 + (2 * j + h + 1))
                        conv_done(j, 4 * h)
                        dve.tensor_tensor(u_pad[:, 2 + h * HALF:2 + (h + 1) * HALF], bank, ccs[:, cols],
                                          ALU.mult).then_inc(conv_s, 1)
                        conv_done(j, 4 * h + 1)
                        dve.tensor_scalar(yc[:, cols], u_pad[:, h * HALF:(h + 1) * HALF], cwc[:, j, 0:1], None,
                                          ALU.mult).then_inc(conv_s, 1)
                        for t in (1, 2):
                            conv_done(j, 4 * h + 1 + t)
                            dve.scalar_tensor_tensor(out=yc[:, cols], in0=u_pad[:, h * HALF + t:(h + 1) * HALF + t],
                                                     scalar=cwc[:, j, t:t + 1], in1=yc[:, cols], op0=ALU.mult,
                                                     op1=ALU.add).then_inc(conv_s, 1)
                    elif kind == "cb":
                        dve.wait_ge(unit_s, done)
                        conv_done(j, 8 + h)
                        dve.tensor_tensor(yc[:, cols], bank, yc[:, cols], ALU.mult).then_inc(conv_s, 1)
                    elif kind == "gc":
                        dve.wait_ge(gc_s, k * 4 + (2 * j + h + 1))
                        conv_done(j, 10 + h)
                        dve.scalar_tensor_tensor(out=res[:, bass.ds(k * 2 + j, 1), cols].rearrange("p a s -> p (a s)"),
                                                 in0=tgc[:, cols], scalar=1.0, in1=yc[:, cols], op0=ALU.add,
                                                 op1=ALU.mult).then_inc(conv_s, 1)
                        if j == 1:
                            conv_done(1, 11 + h)
                            dve.wait_ge(o_s, k * (3 * NB) + (3 * NB if h else 3 * NB // 2))
                            both = res[:, bass.ds(k * 2, 2), cols]
                            dve.tensor_tensor(both, both, tga[:, :, cols], ALU.add).then_inc(merge_s, 1)

                def soft_done(n, step):
                    if SOFT * n + step:
                        dve.wait_ge(soft_s, k * (SOFT * NB) + (SOFT * n + step))

                def softmax(n):
                    lo = P if n == 0 else 0
                    dve.wait_ge(scores_s, k * NB + (n + 1))
                    soft_done(n, 0)
                    dve.scalar_tensor_tensor(out=prob[:, :, lo:], in0=scores_ps[:, :, lo:], scalar=SCALE,
                                             in1=bias[:, :, lo:], op0=ALU.mult, op1=ALU.add).then_inc(soft_s, 1)
                    soft_done(n, 1)
                    dve.tensor_reduce(mx[:], prob[:, :, lo:], AX_X, ALU.max).then_inc(soft_s, 1)
                    soft_done(n, 2)
                    dve.tensor_tensor(mx[:], mx[:], snkc[:], ALU.max).then_inc(soft_s, 1)
                    soft_done(n, 3)
                    dve.tensor_scalar(neg_m[:], mx[:], -1.0, None, ALU.mult).then_inc(soft_s, 1)
                    dve.tensor_tensor(sink_d[:], snkc[:], mx[:], ALU.subtract).then_inc(soft_s, 1)

                def normalise(n):
                    lo = P if n == 0 else 0
                    dve.wait_ge(exp_s, k * (5 * NB) + (5 * n + 5))
                    dve.tensor_tensor(rden[:], rsum[:], sink_e[:], ALU.add).then_inc(soft_s, 1)
                    soft_done(n, 6)
                    dve.reciprocal(rden[:], rden[:]).then_inc(soft_s, 1)
                    soft_done(n, 7)
                    dve.tensor_tensor(prob[:, :, lo:], prob[:, :, lo:],
                                      rden[:].rearrange("p (g o) -> p g o", o=1).broadcast_to([P, G, 2 * P - lo]),
                                      ALU.mult).then_inc(soft_s, 1)

                def gate_attention(n):
                    def o_done(i):
                        if 3 * n + i:
                            dve.wait_ge(o_s, k * (3 * NB) + (3 * n + i))

                    dve.wait_ge(olo_s, k * NB + (n + 1))
                    o_done(0)
                    o_ps = ps[0:HD, OUT, :].rearrange("p (j e q) -> p e j q", j=2, e=2)
                    lo = o_lo[:].rearrange("p (j e q) -> p e j q", j=2, e=2)
                    for e in range(2):
                        dve.tensor_tensor(o_sum[e * HD:(e + 1) * HD], o_ps[:, e], lo[:, e], ALU.add).then_inc(o_s, 1)
                    o_done(2)
                    dve.wait_ge(ga_s, k * 4 + 4)
                    dve.scalar_tensor_tensor(out=tga[:, :, blk(n)], in0=tga[:, :, blk(n)], scalar=1.0,
                                             in1=o_sum[:], op0=ALU.add, op1=ALU.mult).then_inc(o_s, 1)

                for step, n in STEPS:
                    if step == "unit":
                        unit(n)
                    elif step == "scores":
                        softmax(n)
                        normalise(n)
                    elif step == "turn":
                        for kb in range(1 if n == 0 else 0, 2):
                            dve.wait_ge(pt_hi_s, k * NTURN + (turned(n, kb) + 1))
                            dve.tensor_tensor(pt_lo[:, kb], ps[:, TURN + kb, :], fp(pt_hi[:, kb]),
                                              ALU.subtract).then_inc(pt_lo_s, 1)
                    else:
                        gate_attention(n)
                soft_done(NB - 1, SOFT)
                conv_done(1, 12)
                dve.wait_ge(o_s, k * (3 * NB) + 3 * NB)
                dve.wait_ge(merge_s, k * 2 + 2)

            def mixer_low(h, m):
                dve.wait_ge(m_hi_s, DT * h + m + 1)
                dve.scalar_tensor_tensor(out=m_lo[h][:, m], in0=res[:, m, half(h)], scalar=0.5,
                                         in1=fp(m_hi[h][:, m]), op0=ALU.mult, op1=ALU.subtract).then_inc(m_lo_s, 1)

            def x_sum(h, m):
                dve.wait_ge(m_lo_s, DT * h + m + 1)
                dve.tensor_tensor(res[:, m, half(h)], fp(act_hi[:, m, half(h)]), fp(act_lo[:, m, half(h)]),
                                  ALU.add).then_inc(xsum_s, 1)

            def centre(q):
                def odd_squares(m):
                    dve.wait_ge(sq_s, 8 * q + m + 1)
                    if m > 3:
                        dve.wait_ge(odd_s, 3 * q + m // 2 - 1)
                    dve.tensor_tensor(sq_acc[:, 1], sq_acc[:, 1], sq[:, 1], ALU.add).then_inc(odd_s, 1)

                dve.wait_ge(stat_s, 3 * q + 1)
                for m in range(DT):
                    tile = res[:, m, half(q)]
                    dve.tensor_tensor(tile, tile, ps[:, MEAN, :], ALU.subtract).then_inc(cen_s, 1)
                    if m == 5:
                        odd_squares(3)
                odd_squares(5)
                odd_squares(7)

            def invert(q):
                dve.wait_ge(std_s, q + 1)
                dve.reciprocal(inv[:], std[:]).then_inc(inv_s, 1)

            def norm_low(q, m):
                dve.wait_ge(n_hi_s, 8 * q + m + 1)
                dve.scalar_tensor_tensor(out=act_lo[:, m, half(q)], in0=res[:, m, half(q)], scalar=lnb[:, m:m + 1],
                                         in1=fp(act_hi[:, m, half(q)]), op0=ALU.add,
                                         op1=ALU.subtract).then_inc(n_lo_s, 1)

            def normalise_half(q, ms):
                dve.wait_ge(stat_s, 3 * q + 3)
                dve.wait_ge(sq_s, 8 * q + 8)
                for m in ms:
                    tile = res[:, m, half(q)]
                    dve.scalar_tensor_tensor(out=tile, in0=tile, scalar=lng[:, m:m + 1], in1=ps[:, INV, :],
                                             op0=ALU.mult, op1=ALU.mult).then_inc(norm_s, 1)
                    if m > ms[0]:
                        norm_low(q, m - 1)
                norm_low(q, ms[-1])

            def scale_residual(q):
                dve.wait_ge(n_lo_s, 8 * q + 8)
                for m in range(DT):
                    dve.tensor_scalar(res[:, m, half(q)], res[:, m, half(q)], lnb[:, m:m + 1], ALPHA,
                                      ALU.add, ALU.mult).then_inc(scaled_s, 1)

            for m in range(DT):
                mixer_low(0, m)
            dve.memset(acc[:], 0.0).then_inc(res_s, 2)
            for v in range(OUT_TILES):
                h, m = v // DT, v % DT
                if h == 0:
                    x_sum(0, m)
                dve.wait_ge(out_s, v + 1)
                dve.wait_ge(xsum_s, DT * 2 if h else 2 * m + 1)
                dve.scalar_tensor_tensor(out=res[:, m, half(h)], in0=res[:, m, half(h)], scalar=ALPHA,
                                         in1=ps[:, v % 2, :], op0=ALU.mult, op1=ALU.add).then_inc(res_s, 1)
                if h == 0:
                    mixer_low(1, m)
                    x_sum(1, m)
                if v == DT:
                    dve.wait_ge(res_s, 2 + DT)
                    centre(0)
                if v == DT + 1:
                    invert(0)
                    normalise_half(0, range(4))
                if v == DT + 2:
                    normalise_half(0, range(4, DT))
                if v == DT + 3:
                    scale_residual(0)

            def hidden(g, h, t):
                dve.wait_ge(silu_s, g * 8 + (4 * h + 2 * t + 1))
                if h:
                    dve.wait_ge(hid_s, g * 12 + (3 * t + 3))
                dve.scalar_tensor_tensor(out=hid[:, t], in0=tanh_g[:, t], scalar=1.0, in1=ps[:, 2 * t, :],
                                         op0=ALU.add, op1=ALU.mult).then_inc(hid_s, 1)
                dve.wait_ge(f_s, g * 8 + (4 * h + 2 * t + 2))
                dve.wait_ge(hid_s, g * 12 + (6 * h + 3 * t + 1))
                dve.tensor_tensor(hid[:, t], hid[:, t], ps[:, 2 * t + 1, :], ALU.mult).then_inc(hid_s, 1)
                dve.wait_ge(silu_s, g * 8 + (4 * h + 2 * t + 2))
                dve.scalar_tensor_tensor(out=hid_lo[:, t, half(h)], in0=hid[:, t], scalar=0.5,
                                         in1=fp(hid_hi[:, t, half(h)]), op0=ALU.mult,
                                         op1=ALU.subtract).then_inc(hid_s, 1)

            dve.wait_ge(res_s, 2 + OUT_TILES)
            centre(1)
            hidden(0, 0, 0)
            invert(1)
            normalise_half(1, range(DT))
            hidden(0, 0, 1)
            scale_residual(1)
            dve.wait_ge(scaled_s, 2 * DT)

            def add_down(g, v):
                h, m = v // DT, v % DT
                dve.wait_ge(d_s, g * 16 + (v + 1))
                dve.tensor_tensor(res[:, m, half(h)], res[:, m, half(h)], ps[:, 4 + v % 4, :],
                                  ALU.add).then_inc(add_s, 1)

            with dve.Fori(0, NG - 1) as g:
                hidden(g, 1, 0)
                hidden(g, 1, 1)
                for v in range(2 * DT):
                    add_down(g, v)
                dve.wait_ge(add_s, g * 16 + 16)
                dve.wait_ge(hid_s, g * 12 + 12)
                hidden(g + 1, 0, 0)
                hidden(g + 1, 0, 1)
            hidden(NG - 1, 1, 0)
            hidden(NG - 1, 1, 1)

            def row_stats(i):
                k = i % 2
                dve.wait_ge(ot_s, i + 1)
                for b in range(2):
                    dve.bn_stats(bn[:, k, b], row_banks(i)[:, b]).then_inc(bn_s, 1)
                dve.wait_ge(bn_s, 4 * i + 2)
                dve.bn_aggr(mv[:, k], bn[:, k].rearrange("p b s -> p (b s)")).then_inc(bn_s, 1)
                dve.wait_ge(bn_s, 4 * i + 3)
                dve.tensor_scalar(neg_mean[:, k:k + 1], mv[:, k, 0:1], -1.0, None, ALU.mult).then_inc(bn_s, 1)

            def row_scale(i):
                k = i % 2
                dve.wait_ge(std2_s, i + 1)
                dve.reciprocal(inv2[:, k:k + 1], std2[:, k:k + 1]).then_inc(inv2_s, 1)
                dve.wait_ge(rcen_s, i + 1)
                dve.wait_ge(inv2_s, i + 1)
                dve.scalar_tensor_tensor(out=ost[:, i % 4, :], in0=ost[:, i % 4, :], scalar=inv2[:, k:k + 1],
                                         in1=ln2_rows[:, 0, :], op0=ALU.mult, op1=ALU.mult).then_inc(rgam_s, 1)

            dve.wait_ge(rows_in, 32)
            for v in range(DT + 1):
                add_down(NG - 1, v)
            add_down(NG - 1, 9)
            row_stats(0)
            add_down(NG - 1, 10)
            add_down(NG - 1, 11)
            row_stats(1)
            row_scale(0)
            for v in range(12, 14):
                add_down(NG - 1, v)
            row_scale(1)
            for v in range(14, 16):
                add_down(NG - 1, v)
            for i in range(2, NB):
                row_stats(i)
                if i > 2:
                    row_scale(i - 1)
            row_scale(NB - 1)

        @block.tensor
        def _(pe):
            def product(bank, w_h, w_l, a_hi, a_lo, tiles, ready=None):
                for t in range(tiles):
                    if ready is not None:
                        ready(t)
                    pe.matmul(bank, w_h(t), a_hi(t), start=(t == 0), stop=False)
                    pe.matmul(bank, w_h(t), a_lo(t), start=False, stop=False)
                    last = pe.matmul(bank, w_l(t), a_hi(t), start=False, stop=(t == tiles - 1))
                return last

            def project(slot, h, bank, ready=None):
                return product(ps[:, bank, :], lambda t: w_hi[:, slot, t], lambda t: w_lo[:, slot, t],
                               lambda t: act_hi[:, t, half(h)], lambda t: act_lo[:, t, half(h)], DT, ready)

            pe.wait_ge(tables, 2)

            def turn_x(i):
                st, cg = i // 2, i % 2
                pe.wait_ge(x_in[st], 16)
                if i >= 4:
                    pe.wait_ge(x_lo_s, i - 3)
                for c in range(4):
                    last = pe.transpose(ps[:, 4 + i % 4, blk(c)], xs[:, st, blk(4 * cg + c)], ident[:])
                last.then_inc(x_turned, 1)

            def turn_v(i):
                pe.wait_ge(v_copied, i + 1)
                if i >= 2:
                    pe.wait_ge(v_kept, 2 * (i - 1))
                for b in range(4):
                    last = pe.transpose(ps[:, 3 + i % 2, blk(b)], yc[:, (i % 2) * HALF + b * P:(i % 2) * HALF + (b + 1) * P],
                                        ident[:])
                last.then_inc(v_turned, 1)

            for i in range(8):
                turn_x(i)
            for n in range(2 * PRO_TILES):
                t, h = n // 2, n % 2
                if n == 1:
                    for i in range(8, 16):
                        turn_x(i)
                pe.wait_ge(w_lo_s, t + 1)
                pe.wait_ge(x_lo_s, 16 if h else 8)
                if n >= 3:
                    if n - 3 < 4:
                        pe.wait_ge(k_copied, 4 * (n - 2))
                    else:
                        pe.wait_ge(v_copied, n - 6)
                project(t % 2, h, unit_bank(n + 1)).then_inc(unit_s, 1)
                if n >= 5:
                    turn_v(n - 5)
            turn_v(3)

            pe.wait_ge(v_kept, 8)
            with pe.Fori(0, NKV) as k:
                for step, n in STEPS:
                    if step == "unit":
                        if n % 2 == 0:
                            pe.wait_ge(w_lo_s, k * NT + (PRO_TILES + n // 2 + 1))
                        if n == 2:
                            pe.wait_ge(q_hi_s, k * 8 + 2)
                        if n >= 3:
                            pe.wait_ge(*consumed(k, n - 3))
                        project((n // 2) % 2, n % 2, unit_bank(n)).then_inc(unit_s, 1)
                    elif step == "scores":
                        if n == 0:
                            pe.wait_ge(prep_dve, k * 9 + 2)
                            pe.wait_ge(q_lo_s, k * 8 + 8)
                        else:
                            pe.wait_ge(soft_s, k * (SOFT * NB) + (SOFT * (n - 1) + 1))
                        keys = slice(max(n - 1, 0) * P, (n + 1) * P)
                        for g in range(G):
                            dst = scores_ps[:, g, (P if n == 0 else 0):]
                            pe.matmul(dst, q_st[:, g, blk(n)], ks_hi[:, keys], start=True, stop=False)
                            last = pe.matmul(dst, q_st[:, g, blk(n)], ks_lo[:, keys], start=False, stop=True)
                        last.then_inc(scores_s, 1)
                    elif step == "turn":
                        pe.wait_ge(soft_s, k * (SOFT * NB) + (SOFT * n + SOFT))
                        if n:
                            pe.wait_ge(pt_lo_s, k * NTURN + turned(n, 0))
                        for kb in range(1 if n == 0 else 0, 2):
                            for g in range(G):
                                last = pe.transpose(ps[:, TURN + kb, blk(g)], prob[:, g, blk(kb)], ident[:])
                            last.then_inc(turn_s, 1)
                    else:
                        pe.wait_ge(pt_lo_s, k * NTURN + (turned(n, 1) + 1))
                        if n:
                            pe.wait_ge(o_s, k * (3 * NB) + (3 * (n - 1) + 2))
                        kbs = [1] if n == 0 else [0, 1]
                        for kb in kbs:
                            for part in (pt_hi, pt_lo):
                                last = pe.matmul(ps[:, OUT, :], vs[:, n - 1 + kb, :], part[:, kb],
                                                 start=(kb == kbs[0] and part is pt_hi),
                                                 stop=(kb == 1 and part is pt_lo))
                        last.then_inc(values_s, 1)
                pe.wait_ge(conv_s, k * 24 + 22)
                pe.wait_ge(gc_s, k * 4 + 3)
                pe.wait_ge(o_s, k * (3 * NB) + (3 * NB - 1))

            def mean(q):
                pe.wait_ge(acc_s, 7 * (q + 1))
                pe.matmul(ps[:, MEAN, :], mean_of[:], acc[:], start=True, stop=True).then_inc(stat_s, 1)

            def variance(q):
                pe.wait_ge(even_s, 3 * (q + 1))
                pe.wait_ge(odd_s, 3 * (q + 1))
                for b in range(4):
                    for part in range(2):
                        last = pe.matmul(ps[:, VAR, b:b + 1], sq_acc[:, part, blk(b)], mean_of[:, 0:1],
                                         start=(part == 0), stop=(part == 1))
                last.then_inc(stat_s, 1)

            def spread(q):
                pe.wait_ge(inv_s, q + 1)
                for b in range(4):
                    last = pe.matmul(ps[:, INV, blk(b)], inv[:, b:b + 1].broadcast_to([P, P]), ident[:],
                                     start=True, stop=True)
                last.then_inc(stat_s, 1)

            def weave(at, ready=None):
                def hook(t):
                    if ready is not None:
                        ready(t)
                    if t in at:
                        at[t]()
                return hook

            def project_out(h, v, slot, bank, at={}):
                pe.wait_ge(w_lo_s, v + (IN_TILES + 1))
                pe.wait_ge(res_s, v + 1)
                return product(ps[:, bank, :], lambda t: w_hi[:, slot, t], lambda t: w_lo[:, slot, t],
                               lambda t: m_hi[h][:, t], lambda t: m_lo[h][:, t], DT,
                               weave(at, lambda t: pe.wait_ge(m_lo_s, DT * h + t + 1))).then_inc(out_s, 1)

            with pe.Fori(0, DT // 2) as i:
                for e in range(2):
                    project_out(0, i * 2 + e, e, e)
            for v in range(DT, 2 * DT):
                project_out(1, v, v % 2, v % 2, {DT: {4: lambda: mean(0)},
                                                 DT + 2: {1: lambda: variance(0), 4: lambda: spread(0)}}.get(v, {}))

            def gate_up(g, h, s, ready=None):
                if h == 0:
                    pe.wait_ge(fw_lo_s, g * 6 + (s + 1))
                w_h, w_l = ffn_hi(s), ffn_lo(s)
                product(ps[:, s, :], lambda t: w_h[:, t], lambda t: w_l[:, t],
                        lambda t: act_hi[:, t, half(h)], lambda t: act_lo[:, t, half(h)], DT,
                        ready).then_inc(f_s, 1)

            def down(g, h, m):
                v = h * DT + m
                if m == 0:
                    pe.wait_ge(fw_lo_s, g * 6 + 6)
                    pe.wait_ge(hid_s, g * 12 + 6 * (h + 1))
                if v >= 4:
                    pe.wait_ge(add_s, g * 16 + (v - 3))
                product(ps[:, 4 + v % 4, :], lambda t: wd_hi[:, t, blk(m)], lambda t: wd_lo[:, t, blk(m)],
                        lambda t: hid_hi[:, t, half(h)], lambda t: hid_lo[:, t, half(h)], 2).then_inc(d_s, 1)

            pe.wait_ge(n_lo_s, DT)
            pe.wait_ge(res_s, 2 + OUT_TILES)
            gate_up(0, 0, 0, weave({4: lambda: mean(1)}))
            gate_up(0, 0, 1)
            gate_up(0, 0, 2, weave({1: lambda: variance(1), 5: lambda: spread(1)}))
            gate_up(0, 0, 3)

            def second_half(g):
                for s in range(4):
                    pe.wait_ge(hid_s, g * 12 + (3 * (s // 2) + 1 + s % 2))
                    gate_up(g, 1, s, (lambda t: pe.wait_ge(n_lo_s, DT + t + 1)) if s == 0 else None)

            with pe.Fori(0, NG - 1) as g:
                second_half(g)
                for h in range(2):
                    for m in range(DT):
                        down(g, h, m)
                for s in range(4):
                    pe.wait_ge(hid_s, g * 12 + (6 + 3 * (s // 2) + 1 + s % 2))
                    gate_up(g + 1, 0, s)
                pe.wait_ge(add_s, g * 16 + 2 * DT)
            second_half(NG - 1)
            for m in range(DT):
                down(NG - 1, 0, m)

            def turn_rows(i):
                pe.wait_ge(add_s, 16 * (NG - 1) + DT * (i // 4 + 1))
                if i >= 2:
                    pe.wait_ge(rcen_s, max(j for j in range(i) if ROW_BANKS[j] == ROW_BANKS[i]) + 1
                               if ROW_BANKS[i] in ROW_BANKS[:i] else 1)
                for c in range(DT):
                    last = pe.transpose(row_banks(i)[:, c // 4, blk(c % 4)], res[:, c, blk(i)], ident[:])
                last.then_inc(ot_s, 1)

            for m in range(DT):
                down(NG - 1, 1, m)
                if m in (1, 2):
                    turn_rows(m - 1)
            for i in range(2, NB):
                turn_rows(i)


_INS = ["x", "w_in", "conv_w", "attn_sinks", "w_out", "ln1_g", "ln1_b", "w_gate", "w_up", "w_down", "ln2_g", "ln2_b"]


def kernel(**inputs):
    import concourse.bacc as bacc
    from concourse.bass_utils import run_bass_kernel_spmd

    nc = bacc.Bacc("TRN2", target_bir_lowering=False, num_devices=1)
    arrays, args = {}, []
    for name in _INS:
        a = np.ascontiguousarray(inputs[name])
        arrays[f"in_{name}"] = a
        args.append(nc.dram_tensor(f"in_{name}", a.shape, mybir.dt.from_np(a.dtype), kind="ExternalInput").ap())
    out = nc.dram_tensor("out", (1, S, D), F32, kind="ExternalOutput").ap()
    build(nc, *args, out)
    r = run_bass_kernel_spmd(nc, [arrays], core_ids=[0])
    return r.results[0]["out"]
```

```python
from contextlib import ExitStack

import numpy as np

import concourse.bass as bass
from concourse import mybir

F32 = mybir.dt.float32
F32R = mybir.dt.float32r
ALU = mybir.AluOpType
ACT = mybir.ActivationFunctionType
AX_X = mybir.AxisListType.X

P = 128
D = 1024
S = 1024
DT = D // P
HALF = 512
HD = 64
NQ, NKV = 16, 4
G = NQ // NKV
NB = S // P
DFF = 2816
FT = DFF // P
NG = FT // 2
ALPHA = 2.0 ** 0.25
EPS = 1e-5
NEG = -1e30
SCALE = HD ** -0.5

COL_Q, COL_K, COL_V = 0, D, D + NKV * HD
COL_CB = COL_V + NKV * HD
COL_CC, COL_CH, COL_GC, COL_GA = (COL_CB + D * n for n in (1, 2, 3, 4))

PRO_TILES = 4
TILES = [("q", 0), ("q", 1), ("ga", 0), ("ga", 1)] + [(x, j) for j in (0, 1) for x in ("cc", "ch", "gc", "cb")]
PRO_UNITS = [(0, 0), (1, 0), (0, 1), (1, 1), (2, 0), (2, 1), (3, 0), (3, 1)]
NT = len(TILES)
IN_TILES = PRO_TILES + NKV * NT
OUT_TILES = 2 * DT
COLS = {"q": COL_Q, "ga": COL_GA, "cc": COL_CC, "ch": COL_CH, "cb": COL_CB, "gc": COL_GC}


def head_schedule():
    first = 4
    steps = []
    for u in range(2 * NT):
        v = u - first
        if v >= 2 and v % 2 == 0 and (v - 2) // 2 < NB:
            steps.append(("scores", (v - 2) // 2))
        steps.append(("unit", u))
        if v >= 3 and v % 2 == 1 and (v - 3) // 2 < NB:
            steps.append(("turn", (v - 3) // 2))
        if v >= 4 and v % 2 == 0 and (v - 4) // 2 < NB:
            steps.append(("values", (v - 4) // 2))
    return steps


STEPS = head_schedule()

WARM = [26, 4, 4, 4, 0]

LAST = [("unit", 0), ("rows", 0), ("unit", 1), ("silu", 0), ("rows", 1), ("unit", 2), ("rows", 2), ("unit", 3),
        ("silu", 1)] + [("rows", i) for i in range(3, NB)]

SOFT = 8


def turned(n, kb):
    return 0 if n == 0 else 2 * n - 1 + kb


NTURN = 2 * NB - 1


def build(nc, x, w_in, conv_w, sinks, w_out, ln1_g, ln1_b, w_gate, w_up, w_down, ln2_g, ln2_b, out):
    ctx = ExitStack()
    with ctx:
        def sem(name):
            return ctx.enter_context(nc.semaphore(name))

        def sb(stack, name, shape, dt=F32):
            return stack.enter_context(nc.sbuf_tensor(name, shape, dt))

        act_hi = sb(ctx, "act_hi", [P, DT, S], F32R)
        act_lo = sb(ctx, "act_lo", [P, DT, S], F32R)
        res = sb(ctx, "res", [P, DT, S])
        raw = sb(ctx, "raw", [P, 2, DT, P])
        w_hi = sb(ctx, "w_hi", [P, 2, DT, P], F32R)
        w_lo = sb(ctx, "w_lo", [P, 2, DT, P], F32R)
        ident = sb(ctx, "ident", [P, P])
        mean_of = sb(ctx, "mean_of", [P, P])
        cw = sb(ctx, "cw", [P, DT, 3])
        snk = sb(ctx, "snk", [P, NQ])
        lng = sb(ctx, "lng", [P, DT])
        lnb = sb(ctx, "lnb", [P, DT])
        std = sb(ctx, "std", [P, NB // 2])
        inv = sb(ctx, "inv", [P, NB // 2])
        eps = sb(ctx, "eps", [P, 1])
        bn = sb(ctx, "bn", [P, 2, 2, 6])
        mv = sb(ctx, "mv", [P, 2, 2])
        neg_mean = sb(ctx, "neg_mean", [P, 2])
        std2 = sb(ctx, "std2", [P, 2])
        inv2 = sb(ctx, "inv2", [P, 2])

        with ExitStack() as st:
            q_st = sb(st, "q_st", [P, G, S], F32R)
            pt_hi = sb(st, "pt_hi", [P, 2, G * P], F32R)
            pt_lo = sb(st, "pt_lo", [P, 2, G * P], F32R)
            prob = sb(st, "prob", [P, G, 2 * P])
            ks_hi = sb(st, "ks_hi", [P, S], F32R)
            ks_lo = sb(st, "ks_lo", [P, S], F32R)
            vs = sb(st, "vs", [P, NB, 2 * HD], F32R)
            bias = sb(st, "bias", [P, G, 2 * P])
            negdist = sb(st, "negdist", [P, 2 * P])
            mask = sb(st, "mask", [P, 2 * P])
            ccs = sb(st, "ccs", [P, S])
            tga = sb(st, "tga", [P, 2, S])
            slope = sb(st, "slope", [P, G])
            snkc = sb(st, "snkc", [P, G])
            cwc = sb(st, "cwc", [P, 2, 3])
            u_pad = sb(st, "u_pad", [P, 2 + S])
            yc = sb(st, "yc", [P, S])
            tgc = sb(st, "tgc", [P, S])
            o_lo = sb(st, "o_lo", [HD, G * P])
            o_sum = sb(st, "o_sum", [P, 2, P])
            mx = sb(st, "mx", [P, G])
            neg_m = sb(st, "neg_m", [P, G])
            sink_d = sb(st, "sink_d", [P, G])
            sink_e = sb(st, "sink_e", [P, G])
            rsum = sb(st, "rsum", [P, G])
            rden = sb(st, "rden", [P, G])
        with ExitStack() as st:
            xs = sb(st, "xs", [P, NB, D])

        late = ctx.enter_context(ExitStack())
        with ExitStack() as st:
            acc = sb(st, "acc", [P, HALF])
            sq_acc = sb(st, "sq_acc", [P, 2, HALF])
            sq = sb(st, "sq", [P, 2, HALF])
        ln2_rows = sb(late, "ln2_rows", [P, 2, D])
        sb(late, "spare", [P, HALF])
        raw_b = sb(late, "raw_b", [P, 2, DT, P])
        with ExitStack() as st:
            m_hi, m_lo = [], []
            for h in range(2):
                m_hi.append(sb(st, f"m_hi{h}", [P, DT, HALF], F32R))
                m_lo.append(sb(st, f"m_lo{h}", [P, DT, HALF], F32R))
        with ExitStack() as st:
            w_hi_b = sb(st, "w_hi_b", [P, 2, DT, P], F32R)
            w_lo_b = sb(st, "w_lo_b", [P, 2, DT, P], F32R)
            wd_hi = sb(st, "wd_hi", [P, 2, D], F32R)
            wd_lo = sb(st, "wd_lo", [P, 2, D], F32R)
            raw_d = sb(st, "raw_d", [P, 2, D])
            hid_hi = sb(st, "hid_hi", [P, 2, S], F32R)
            hid_lo = sb(st, "hid_lo", [P, 2, S], F32R)
            tanh_g = sb(st, "tanh_g", [P, 2, HALF])
            hid = sb(st, "hid", [P, 2, HALF])

        ps = ctx.enter_context(nc.psum_tensor("ps", [P, 8, HALF], F32))
        SCORE, TURN, OUT = 3, 5, 7
        scores_ps = ps[:, SCORE:SCORE + 2, :].rearrange("p b (g k) -> p (b g) k", k=2 * P)

        x_in = [sem(f"x_in{i}") for i in range(NB)]
        params_in = sem("params_in")
        w_in_s = [sem(f"w_landed{i}") for i in range(2)]
        tables = sem("tables")
        x_turned, x_hi_s, x_lo_s = sem("x_turned"), sem("x_hi_done"), sem("x_lo_done")
        w_hi_s, w_lo_s = sem("w_hi_done"), sem("w_lo_done")
        unit_s = sem("unit_done")
        k_copied, v_copied, v_turned, v_kept = sem("k_copied"), sem("v_copied"), sem("v_turned"), sem("v_kept")
        prep_act, prep_dve = sem("head_prep_act"), sem("head_prep_dve")
        q_hi_s, q_lo_s = sem("q_hi_done"), sem("q_lo_done")
        ga_s, cc_s, gc_s = sem("ga_tanh_done"), sem("cc_copied"), sem("gc_tanh_done")
        conv_s = sem("conv_step")
        scores_s, soft_s, exp_s = sem("scores_done"), sem("softmax_step"), sem("exp_done")
        turn_s, pt_hi_s, pt_lo_s = sem("probs_turned"), sem("pt_hi_done"), sem("pt_lo_done")
        values_s, olo_s, o_s = sem("values_done"), sem("o_lo_copied"), sem("o_step")
        merge_s = sem("merge_done")
        m_hi_s, m_lo_s, xsum_s = sem("m_hi_done"), sem("m_lo_done"), sem("x_sum_done")
        out_s, res_s = sem("out_unit_done"), sem("res_tile_done")
        acc_s, cen_s, sq_s = sem("channel_sum_step"), sem("centred"), sem("squared")
        even_s, odd_s, stat_s = sem("even_squares_step"), sem("odd_squares_step"), sem("stat_done")
        std_s, inv_s, norm_s = sem("std_done"), sem("inverse_done"), sem("normalised")
        n_hi_s, n_lo_s, scaled_s = sem("norm_hi_done"), sem("norm_lo_done"), sem("residual_scaled")
        fw_in = [sem(f"ffn_w_landed{i}") for i in range(6)]
        fw_hi_s, fw_lo_s = sem("ffn_w_hi_done"), sem("ffn_w_lo_done")
        f_s, d_s = sem("gate_up_unit_done"), sem("down_unit_done")
        silu_s, hid_s, add_s = sem("silu_act_step"), sem("hidden_step"), sem("down_added")
        rows_in = sem("ln2_rows_in")
        ot_s, bn_s, std2_s, inv2_s = sem("rows_turned"), sem("row_stats_step"), sem("row_std_done"), sem("row_inverse_done")
        rcen_s, rgam_s, rout_s = sem("rows_centred"), sem("rows_scaled"), sem("rows_done")
        last_s = sem("last_half_row_done")
        stored = [sem(f"stored{i}") for i in range(4)]

        block = ctx.enter_context(nc.Block())

        def half(h):
            return slice(h * HALF, (h + 1) * HALF)

        def blk(n):
            return slice(n * P, (n + 1) * P)

        def fp(ap):
            return ap.bitcast(F32)

        def unit_bank(u):
            return u % 3

        def consumed(k, u):
            kind, j = TILES[u // 2]
            h = u % 2
            if kind == "q":
                return q_lo_s, 8 * k + 4 * j + 2 * h + 2
            if kind == "ga":
                return ga_s, 4 * k + 2 * j + h + 1
            if kind == "cc":
                return cc_s, 4 * k + 2 * j + h + 1
            if kind == "gc":
                return gc_s, 4 * k + 2 * j + h + 1
            return conv_s, 24 * k + 12 * j + (4 * h + 1 if kind == "ch" else 11 + h)

        def ffn_raw(s):
            return raw_b[:, s] if s < 2 else raw[:, s - 2] if s < 4 else raw_d[:, s - 4]

        def ffn_hi(s):
            return w_hi_b[:, s] if s < 2 else w_hi[:, s - 2] if s < 4 else wd_hi[:, s - 4]

        def ffn_lo(s):
            return w_lo_b[:, s] if s < 2 else w_lo[:, s - 2] if s < 4 else wd_lo[:, s - 4]

        def out_slot(v):
            return 4 + v % 2 if v in (10, 11, 14, 15) else 2 + v % 2

        def out_slot_free(v):
            return v - 1 if v < 10 else DT if v < 12 else v - 3

        def out_hi(v):
            hi = ffn_hi(out_slot(v))
            return hi if v not in (10, 11, 14, 15) else hi.rearrange("p (t c) -> p t c", c=P)

        def out_lo(v):
            lo = ffn_lo(out_slot(v))
            return lo if v not in (10, 11, 14, 15) else lo.rearrange("p (t c) -> p t c", c=P)

        OB = 4
        MEAN, VAR, INV = 6, 7, 5
        ROW_BANKS = [4, 6, 4, 6, 0, 2, 4, 6]

        def row_out(i):
            return raw_b[:, i % 4].rearrange("p t c -> p (t c)") if i % 4 < 2 else raw_d[:, i % 4 - 2]

        def row_banks(i):
            return ps[:, ROW_BANKS[i]:ROW_BANKS[i] + 2, :]

        @block.sync
        def _(sp):
            def load_w(tile_slot, w, col):
                src = w[0, :, bass.ds(col, P)].rearrange("(t p) c -> p t c", p=P)
                sp.dma_start(raw[:, tile_slot], src).then_inc(w_in_s[tile_slot], 16)

            for i in range(NB):
                sp.dma_start(xs[:, i, :], x[0, blk(i), :]).then_inc(x_in[i], 16)
                if i in (0, 3):
                    load_w(i // 3, w_in, COL_V + P * (i // 3))
            with nc.allow_non_contiguous_dma(reason="per-channel parameters, loaded once"):
                sp.dma_start(snk[:], sinks[0:1, :].partition_broadcast(P)).then_inc(params_in, 16)
                for t in range(3):
                    sp.dma_start(cw[:, :, t], conv_w[0, t].rearrange("(m p) -> p m", p=P)).then_inc(params_in, 16)
                for dst, src in ((lng, ln1_g), (lnb, ln1_b)):
                    sp.dma_start(dst[:], src[0].rearrange("(m p) -> p m", p=P)).then_inc(params_in, 16)
            for t in (2, 3):
                sp.wait_ge(w_lo_s, t - 1)
                load_w(t % 2, w_in, COL_K + P * (t - 2))
            with sp.Fori(0, NKV) as k:
                for i, (kind, j) in enumerate(TILES):
                    sp.wait_ge(w_lo_s, k * NT + (PRO_TILES + i - 1))
                    load_w(i % 2, w_in, k * (2 * P) + (COLS[kind] + P * j))
            def load_ffn(g, s):
                if s < 4:
                    w = (w_gate, w_up)[s % 2]
                    src = w[0, :, bass.ds(g * (2 * P) + P * (s // 2), P)].rearrange("(t p) c -> p t c", p=P)
                else:
                    src = w_down[0, bass.ds(g * (2 * P) + P * (s - 4), P), :]
                sp.dma_start(ffn_raw(s), src).then_inc(fw_in[s], 16)

            for v in range(OUT_TILES):
                sp.wait_ge(w_lo_s, IN_TILES + v - 1)
                load_w(v % 2, w_out, P * (v % DT))
                if v == DT:
                    sp.wait_ge(merge_s, 2 * NKV)
                    load_ffn(0, 0)
                    load_ffn(0, 1)
            for s in (2, 3):
                sp.wait_ge(w_lo_s, IN_TILES + OUT_TILES - 3 + s)
                load_ffn(0, s)
            sp.wait_ge(out_s, OUT_TILES)
            load_ffn(0, 4)
            load_ffn(0, 5)
            with sp.Fori(1, NG) as g:
                for s in range(6):
                    sp.wait_ge(fw_lo_s, g * 6 + (s - 5))
                    load_ffn(g, s)
            sp.wait_ge(scaled_s, 2 * DT)
            for n, row in enumerate((ln2_g, ln2_b)):
                sp.dma_start(ln2_rows[:, n, :], row[0:1, :].partition_broadcast(P)).then_inc(rows_in, 16)
            for i in range(NB - 1):
                sp.wait_ge(rout_s, i + 1)
                sp.dma_start(out[0, blk(i), :], row_out(i)).then_inc(stored[i % 4], 16)
            i = NB - 1
            for b, half_done in enumerate((rout_s, last_s)):
                sp.wait_ge(half_done, NB if b == 0 else 1)
                sp.dma_start(out[0, blk(i), half(b)], row_out(i)[:, half(b)]).then_inc(stored[i % 4], 16)
            for i in range(4):
                sp.wait_ge(stored[i], 16 * (NB // 4 + (i == 3)))

        @block.gpsimd
        def _(pool):
            pool.memset(ident[:], 0.0).then_inc(tables, 1)
            pool.wait_ge(tables, 1)
            pool.affine_select(out=ident[:], in_=ident[:], compare_op=ALU.not_equal, fill=1.0, base=0,
                               pattern=[[-1, P]], channel_multiplier=1).then_inc(tables, 1)
            pool.memset(mean_of[:], 1.0 / D).then_inc(tables, 1)
            pool.memset(eps[:], EPS).then_inc(tables, 1)
            pool.memset(u_pad[:, 0:2], 0.0).then_inc(tables, 1)
            pool.iota(negdist[:], pattern=[[1, 2 * P]], base=-P, channel_multiplier=-1,
                      allow_small_or_imprecise_dtypes=True).then_inc(tables, 1)
            pool.memset(mask[:], 0.0).then_inc(tables, 1)
            pool.wait_ge(tables, 7)
            pool.affine_select(out=mask[:], in_=mask[:], compare_op=ALU.is_ge, fill=NEG, base=P,
                               pattern=[[-1, 2 * P]], channel_multiplier=1).then_inc(tables, 1)
            pool.wait_ge(tables, 8)
            pool.affine_select(out=mask[:], in_=mask[:], compare_op=ALU.is_ge, fill=NEG, base=-1,
                               pattern=[[1, 2 * P]], channel_multiplier=-1).then_inc(tables, 1)
            for g in range(G):
                pool.memset(slope[:, g:g + 1], float(np.float32(2.0 ** (-8.0 * (g + 1) / NQ)))).then_inc(tables, 1)

            def low_part(count, slot):
                pool.wait_ge(w_hi_s, count)
                pool.tensor_tensor(w_lo[:, slot], raw[:, slot], fp(w_hi[:, slot]), ALU.subtract).then_inc(w_lo_s, 1)

            for t in range(6):
                low_part(t + 1, t % 2)
            def merge(k, h):
                pool.wait_ge(conv_s, k * 24 + (23 + h))
                pool.wait_ge(o_s, k * (3 * NB) + (3 * NB // 2) * (h + 1))
                both = res[:, bass.ds(k * 2, 2), half(h)]
                pool.tensor_tensor(both, both, tga[:, :, half(h)], ALU.add).then_inc(merge_s, 1)

            with pool.Fori(0, NKV) as k:
                for i in range(NT):
                    low_part(k * NT + (6 + i + 1), i % 2)
                    if i == NT - 2:
                        merge(k, 0)
                merge(k, 1)

            def ffn_low_part(g, s):
                pool.wait_ge(fw_hi_s, g * 6 + (s + 1))
                pool.tensor_tensor(ffn_lo(s), ffn_raw(s), fp(ffn_hi(s)), ALU.subtract).then_inc(fw_lo_s, 1)

            def channel_sum(q, m):
                if m == 0:
                    return
                pool.wait_ge(res_s, OB + DT * q + m + 1)
                first = res[:, 0, half(q)] if m == 1 else acc[:]
                if m == 1:
                    if q:
                        pool.wait_ge(stat_s, 1)
                else:
                    pool.wait_ge(acc_s, 7 * q + m - 1)
                pool.tensor_tensor(acc[:], first, res[:, m, half(q)], ALU.add).then_inc(acc_s, 1)

            def even_squares(q):
                for m in (2, 4, 6):
                    pool.wait_ge(sq_s, 8 * q + m + 1)
                    if m > 2:
                        pool.wait_ge(even_s, 3 * q + m // 2 - 1)
                    pool.tensor_tensor(sq_acc[:, 0], sq_acc[:, 0], sq[:, 0], ALU.add).then_inc(even_s, 1)

            def out_low_part(v):
                pool.wait_ge(w_hi_s, IN_TILES + v + 1)
                pool.tensor_tensor(out_lo(v), raw[:, v % 2], fp(out_hi(v)), ALU.subtract).then_inc(w_lo_s, 1)

            for v in range(DT):
                out_low_part(v + 2)
                channel_sum(0, v)
            for v in (10, 11):
                out_low_part(v)
            even_squares(0)
            for v in (12, 13):
                out_low_part(v)
            ffn_low_part(0, 0)
            for v in range(3):
                channel_sum(1, v)
            out_low_part(14)
            channel_sum(1, 3)
            out_low_part(15)
            channel_sum(1, 4)
            ffn_low_part(0, 1)
            channel_sum(1, 5)
            ffn_low_part(0, 2)
            channel_sum(1, 6)
            channel_sum(1, 7)
            ffn_low_part(0, 3)
            even_squares(1)
            ffn_low_part(0, 4)
            ffn_low_part(0, 5)
            with pool.Fori(1, NG) as g:
                for s in range(6):
                    ffn_low_part(g, s)
            pool.wait_ge(rows_in, 32)
            for i in range(NB):
                cols = slice(0, HALF if i == NB - 1 else D)
                pool.wait_ge(rgam_s, i + 1)
                pool.tensor_tensor(row_out(i)[:, cols], row_out(i)[:, cols], ln2_rows[:, 1, cols],
                                   ALU.add).then_inc(rout_s, 1)

        @block.scalar
        def _(act):
            def high_part(landed, slot, free, count):
                act.wait_ge(w_in_s[slot], landed)
                if free is not None:
                    act.wait_ge(free, count)
                act.activation(w_hi[:, slot], raw[:, slot], ACT.Copy).then_inc(w_hi_s, 1)

            def x_high(i):
                act.wait_ge(x_turned, i + 1)
                st, cg = i // 2, i % 2
                act.activation(act_hi[:, 4 * cg:4 * cg + 4, blk(st)],
                               ps[:, 4 + i % 4, :].rearrange("p (c s) -> p c s", c=4), ACT.Copy).then_inc(x_hi_s, 1)

            for i in range(16):
                x_high(i)
                if i == 1:
                    high_part(16, 0, None, 0)
                if i == 7:
                    high_part(16, 1, None, 0)
            for n, (t, h) in enumerate(PRO_UNITS):
                act.wait_ge(unit_s, n + 1)
                bank = ps[:, unit_bank(n + 1), :]
                if t < 2:
                    if n >= 2:
                        act.wait_ge(v_turned, n - 1)
                    act.activation(yc[:, half(n % 2)], bank, ACT.Copy).then_inc(v_copied, 1)
                else:
                    j = t - 2
                    for e in range(2):
                        for to in range(2):
                            act.activation(res[to * HD:(to + 1) * HD, 2 * (2 * j + e), half(h)],
                                           bank[e * HD:(e + 1) * HD, :], ACT.Copy).then_inc(k_copied, 1)
                if (t, h) in ((0, 1), (1, 1), (2, 1)):
                    high_part(16 * ((t + 2) // 2 + 1), t % 2, unit_s, n + 1)

            act.wait_ge(v_kept, 8)
            act.wait_ge(k_copied, 16)
            with act.Fori(0, NKV) as k:
                high_part(k * (16 * NT // 2) + 16 * ((PRO_TILES + 1) // 2 + 1), 1, unit_s,
                          k * (2 * NT) + 2 * PRO_TILES)
                act.activation(ks_hi[:], res[:, bass.ds(k * 2, 1), :].rearrange("p a s -> p (a s)"), ACT.Copy).then_inc(prep_act, 1)
                act.activation(vs[:, :, 0:HD],
                               res[:, bass.ds(k * 2 + 1, 1), 0:NB * HD].rearrange("p a (b d) -> p (a b) d", b=NB),
                               ACT.Copy).then_inc(prep_act, 1)
                for step, n in STEPS:
                    if step == "unit":
                        kind, j = TILES[n // 2]
                        h = n % 2
                        bank = ps[:, unit_bank(n), :]
                        done = k * (2 * NT) + (2 * PRO_TILES + n + 1)
                        if kind in ("q", "ga", "cc", "gc"):
                            act.wait_ge(unit_s, done)
                        if kind == "q":
                            for e in range(2):
                                rows = slice(e * HD, (e + 1) * HD)
                                act.activation(q_st[rows, 2 * j + e, half(h)], bank[rows, :],
                                               ACT.Copy).then_inc(q_hi_s, 1)
                        elif kind == "ga":
                            act.activation(tga[:, j, half(h)], bank, ACT.Tanh, scale=0.5).then_inc(ga_s, 1)
                        elif kind == "cc":
                            if j:
                                act.wait_ge(conv_s, k * 24 + 12)
                            act.activation(ccs[:, half(h)], bank, ACT.Copy).then_inc(cc_s, 1)
                        elif kind == "gc":
                            if j:
                                act.wait_ge(conv_s, k * 24 + 10)
                            act.activation(tgc[:, half(h)], bank, ACT.Tanh, scale=0.5).then_inc(gc_s, 1)
                        if h == 1 and n < 2 * NT - 1:
                            i = n // 2
                            high_part(k * (16 * NT // 2) + 16 * ((PRO_TILES + i + 2) // 2 + 1), i % 2, unit_s, done)
                    elif step == "scores":
                        lo = P if n == 0 else 0
                        act.wait_ge(soft_s, k * (SOFT * NB) + (SOFT * n + 5))
                        act.activation(sink_e[:], sink_d[:], ACT.Exp).then_inc(exp_s, 1)
                        for g in range(G):
                            act.activation(prob[:, g, lo:], prob[:, g, lo:], ACT.Exp, bias=neg_m[:, g:g + 1],
                                           accum_out=rsum[:, g:g + 1]).then_inc(exp_s, 1)
                    elif step == "turn":
                        for kb in range(1 if n == 0 else 0, 2):
                            i = k * NTURN + (turned(n, kb) + 1)
                            act.wait_ge(turn_s, i)
                            act.activation(pt_hi[:, kb], ps[:, TURN + kb, :], ACT.Copy).then_inc(pt_hi_s, 1)
                    else:
                        act.wait_ge(values_s, k * NB + (n + 1))
                        if n:
                            act.wait_ge(o_s, k * (3 * NB) + 3 * n)
                        act.activation(o_lo[:], ps[HD:P, OUT, :], ACT.Copy).then_inc(olo_s, 1)
                act.wait_ge(merge_s, k * 2 + 1)

            def mixer_high(h, m):
                act.activation(m_hi[h][:, m], res[:, m, half(h)], ACT.Copy, scale=0.5).then_inc(m_hi_s, 1)

            act.wait_ge(merge_s, 2 * NKV - 1)
            for m in range(DT):
                mixer_high(0, m)
            high_part(16 * ((IN_TILES + 1) // 2 + 1), 1, unit_s, 2 * IN_TILES)
            act.wait_ge(merge_s, 2 * NKV)
            for m in range(4):
                mixer_high(1, m)

            def ffn_high_part(g, s, free, count):
                act.wait_ge(fw_in[s], (g + 1) * 16)
                act.wait_ge(free, count)
                act.activation(ffn_hi(s), ffn_raw(s), ACT.Copy).then_inc(fw_hi_s, 1)

            def squares(q, ms=range(DT)):
                for m in ms:
                    act.wait_ge(cen_s, 8 * q + m + 1)
                    if m >= 2 and 3 * q + (m - 2) // 2:
                        act.wait_ge((even_s, odd_s)[m % 2], 3 * q + (m - 2) // 2)
                    dst = sq_acc[:, m] if m < 2 else sq[:, m % 2]
                    act.activation(dst, res[:, m, half(q)], ACT.Square).then_inc(sq_s, 1)

            def root(q):
                act.wait_ge(stat_s, 3 * q + 2)
                act.activation(std[:], ps[:, VAR, 0:4], ACT.Sqrt, bias=eps[:]).then_inc(std_s, 1)

            def norm_high(q, ms):
                for m in ms:
                    act.wait_ge(norm_s, 8 * q + m + 1)
                    act.activation(act_hi[:, m, half(q)], res[:, m, half(q)], ACT.Identity,
                                   bias=lnb[:, m:m + 1]).then_inc(n_hi_s, 1)

            def out_high_part(v):
                act.wait_ge(w_in_s[v % 2], 16 * ((IN_TILES + v) // 2 + 1))
                act.wait_ge(out_s, out_slot_free(v))
                act.activation(out_hi(v), raw[:, v % 2], ACT.Copy).then_inc(w_hi_s, 1)

            act.wait_ge(params_in, 16 * 6)
            out_high_part(2)
            for m in range(4, DT):
                mixer_high(1, m)
            for v in range(3, 12):
                out_high_part(v)
            squares(0, range(4))
            out_high_part(12)
            squares(0, range(4, DT))
            out_high_part(13)
            root(0)
            ffn_high_part(0, 0, out_s, DT)
            out_high_part(14)
            out_high_part(15)
            norm_high(0, range(4))
            ffn_high_part(0, 1, out_s, DT)
            norm_high(0, range(4, DT))
            ffn_high_part(0, 2, out_s, 13)
            ffn_high_part(0, 3, out_s, 14)

            def silu(g, h, t):
                act.wait_ge(f_s, g * 8 + (4 * h + 2 * t + 1))
                if h:
                    act.wait_ge(hid_s, g * 12 + (3 * t + 1))
                act.activation(tanh_g[:, t], ps[:, 2 * t, :], ACT.Tanh, scale=0.5).then_inc(silu_s, 1)
                act.wait_ge(hid_s, g * 12 + (6 * h + 3 * t + 2))
                act.activation(hid_hi[:, t, half(h)], hid[:, t], ACT.Copy, scale=0.5).then_inc(silu_s, 1)

            squares(1)
            silu(0, 0, 0)
            root(1)
            norm_high(1, range(DT))
            silu(0, 0, 1)
            ffn_high_part(0, 4, out_s, OUT_TILES)
            ffn_high_part(0, 5, out_s, OUT_TILES)

            with act.Fori(0, NG - 1) as g:
                silu(g, 1, 0)
                silu(g, 1, 1)
                for s in range(4):
                    ffn_high_part(g + 1, s, f_s, g * 8 + 8)
                for s in (4, 5):
                    ffn_high_part(g + 1, s, d_s, g * 16 + 16)
                act.wait_ge(hid_s, g * 12 + 12)
                silu(g + 1, 0, 0)
                silu(g + 1, 0, 1)

            def row_centre(i):
                act.wait_ge(bn_s, 4 * i + 3)
                act.activation(std2[:, i % 2:i % 2 + 1], mv[:, i % 2, 1:2], ACT.Sqrt, bias=eps[:]).then_inc(std2_s, 1)
                act.wait_ge(bn_s, 4 * i + 4)
                if i >= 4:
                    act.wait_ge(stored[i % 4], 16 * (i // 4))
                for bs in ((0, 2),) if i < NB - 1 else ((0, 1), (1, 2)):
                    cols = slice(bs[0] * HALF, bs[1] * HALF)
                    act.activation(row_out(i)[:, cols].rearrange("p (b s) -> p b s", s=HALF),
                                   row_banks(i)[:, bs[0]:bs[1]], ACT.Identity,
                                   bias=neg_mean[:, i % 2:i % 2 + 1]).then_inc(rcen_s, 1)

            for step, n in LAST:
                if step == "silu":
                    silu(NG - 1, 1, n)
                elif step == "rows":
                    row_centre(n)

        @block.vector
        def _(dve):
            dve.wait_ge(tables, 13)
            for i in range(16):
                dve.wait_ge(x_hi_s, i + 1)
                st, cg = i // 2, i % 2
                dst = (slice(None), slice(4 * cg, 4 * cg + 4), blk(st))
                dve.tensor_tensor(act_lo[dst], ps[:, 4 + i % 4, :].rearrange("p (c s) -> p c s", c=4),
                                  fp(act_hi[dst]), ALU.subtract).then_inc(x_lo_s, 1)
            for i in range(4):
                j, h = PRO_UNITS[i]
                dve.wait_ge(v_turned, i + 1)
                src = ps[:, 3 + i % 2, :].rearrange("p (b e d) -> p e b d", b=4, e=2)
                for e in range(2):
                    dst = res[:, 2 * (2 * j + e) + 1, 4 * HD * h:4 * HD * (h + 1)].rearrange("p (b d) -> p b d", b=4)
                    dve.tensor_copy(dst, src[:, e]).then_inc(v_kept, 1)
            dve.wait_ge(params_in, 16 * 6)

            with dve.Fori(0, NKV) as k:
                def prep_done(n):
                    dve.wait_ge(prep_dve, k * 9 + n)

                dve.wait_ge(prep_act, k * 2 + 1)
                dve.tensor_tensor(ks_lo[:], res[:, bass.ds(k * 2, 1), :].rearrange("p a s -> p (a s)"),
                                  fp(ks_hi[:]), ALU.subtract).then_inc(prep_dve, 1)
                dve.wait_ge(prep_act, k * 2 + 2)
                dve.tensor_tensor(vs[:, :, HD:2 * HD],
                                  res[:, bass.ds(k * 2 + 1, 1), 0:NB * HD].rearrange("p a (b d) -> p (a b) d", b=NB),
                                  fp(vs[:, :, 0:HD]), ALU.subtract).then_inc(prep_dve, 1)
                for g in range(G):
                    dve.scalar_tensor_tensor(out=bias[:, g], in0=negdist[:], scalar=slope[:, g:g + 1], in1=mask[:],
                                             op0=ALU.mult, op1=ALU.add).then_inc(prep_dve, 1)
                prep_done(6)
                dve.tensor_scalar(slope[:], slope[:], 2.0 ** (-8.0 * G / NQ), None, ALU.mult).then_inc(prep_dve, 1)
                dve.tensor_copy(snkc[:], snk[:, bass.ds(k * G, G)]).then_inc(prep_dve, 1)
                dve.tensor_copy(cwc[:], cw[:, bass.ds(k * 2, 2), :]).then_inc(prep_dve, 1)
                prep_done(9)

                def conv_done(j, n):
                    if 12 * j + n:
                        dve.wait_ge(conv_s, k * 24 + (12 * j + n))

                def unit(n):
                    kind, j = TILES[n // 2]
                    h = n % 2
                    bank = ps[:, unit_bank(n), :]
                    done = k * (2 * NT) + (2 * PRO_TILES + n + 1)
                    cols = half(h)
                    if kind == "q":
                        for e in range(2):
                            rows, other = slice(e * HD, (e + 1) * HD), slice((1 - e) * HD, (2 - e) * HD)
                            dve.wait_ge(q_hi_s, k * 8 + (4 * j + 2 * h + 2))
                            dve.tensor_tensor(q_st[other, 2 * j + e, cols], bank[rows, :],
                                              fp(q_st[rows, 2 * j + e, cols]), ALU.subtract).then_inc(q_lo_s, 1)
                    elif kind == "ch":
                        dve.wait_ge(unit_s, done)
                        dve.wait_ge(cc_s, k * 4 + (2 * j + h + 1))
                        conv_done(j, 4 * h)
                        dve.tensor_tensor(u_pad[:, 2 + h * HALF:2 + (h + 1) * HALF], bank, ccs[:, cols],
                                          ALU.mult).then_inc(conv_s, 1)
                        conv_done(j, 4 * h + 1)
                        dve.tensor_scalar(yc[:, cols], u_pad[:, h * HALF:(h + 1) * HALF], cwc[:, j, 0:1], None,
                                          ALU.mult).then_inc(conv_s, 1)
                        for t in (1, 2):
                            conv_done(j, 4 * h + 1 + t)
                            dve.scalar_tensor_tensor(out=yc[:, cols], in0=u_pad[:, h * HALF + t:(h + 1) * HALF + t],
                                                     scalar=cwc[:, j, t:t + 1], in1=yc[:, cols], op0=ALU.mult,
                                                     op1=ALU.add).then_inc(conv_s, 1)
                    elif kind == "gc":
                        dve.wait_ge(gc_s, k * 4 + (2 * j + h + 1))
                        conv_done(j, 8 + h)
                        dve.scalar_tensor_tensor(out=yc[:, cols], in0=tgc[:, cols], scalar=1.0, in1=yc[:, cols],
                                                 op0=ALU.add, op1=ALU.mult).then_inc(conv_s, 1)
                    elif kind == "cb":
                        dve.wait_ge(unit_s, done)
                        conv_done(j, 10 + h)
                        dve.tensor_tensor(res[:, bass.ds(k * 2 + j, 1), cols].rearrange("p a s -> p (a s)"), bank,
                                          yc[:, cols], ALU.mult).then_inc(conv_s, 1)

                def soft_done(n, step):
                    if SOFT * n + step:
                        dve.wait_ge(soft_s, k * (SOFT * NB) + (SOFT * n + step))

                def softmax(n):
                    lo = P if n == 0 else 0
                    dve.wait_ge(scores_s, k * NB + (n + 1))
                    soft_done(n, 0)
                    dve.scalar_tensor_tensor(out=prob[:, :, lo:], in0=scores_ps[:, :, lo:], scalar=SCALE,
                                             in1=bias[:, :, lo:], op0=ALU.mult, op1=ALU.add).then_inc(soft_s, 1)
                    soft_done(n, 1)
                    dve.tensor_reduce(mx[:], prob[:, :, lo:], AX_X, ALU.max).then_inc(soft_s, 1)
                    soft_done(n, 2)
                    dve.tensor_tensor(mx[:], mx[:], snkc[:], ALU.max).then_inc(soft_s, 1)
                    soft_done(n, 3)
                    dve.tensor_scalar(neg_m[:], mx[:], -1.0, None, ALU.mult).then_inc(soft_s, 1)
                    dve.tensor_tensor(sink_d[:], snkc[:], mx[:], ALU.subtract).then_inc(soft_s, 1)

                def normalise(n):
                    lo = P if n == 0 else 0
                    dve.wait_ge(exp_s, k * (5 * NB) + (5 * n + 5))
                    dve.tensor_tensor(rden[:], rsum[:], sink_e[:], ALU.add).then_inc(soft_s, 1)
                    soft_done(n, 6)
                    dve.reciprocal(rden[:], rden[:]).then_inc(soft_s, 1)
                    soft_done(n, 7)
                    dve.tensor_tensor(prob[:, :, lo:], prob[:, :, lo:],
                                      rden[:].rearrange("p (g o) -> p g o", o=1).broadcast_to([P, G, 2 * P - lo]),
                                      ALU.mult).then_inc(soft_s, 1)

                def gate_attention(n):
                    def o_done(i):
                        if 3 * n + i:
                            dve.wait_ge(o_s, k * (3 * NB) + (3 * n + i))

                    dve.wait_ge(olo_s, k * NB + (n + 1))
                    o_done(0)
                    o_ps = ps[0:HD, OUT, :].rearrange("p (j e q) -> p e j q", j=2, e=2)
                    lo = o_lo[:].rearrange("p (j e q) -> p e j q", j=2, e=2)
                    for e in range(2):
                        dve.tensor_tensor(o_sum[e * HD:(e + 1) * HD], o_ps[:, e], lo[:, e], ALU.add).then_inc(o_s, 1)
                    o_done(2)
                    dve.wait_ge(ga_s, k * 4 + 4)
                    dve.scalar_tensor_tensor(out=tga[:, :, blk(n)], in0=tga[:, :, blk(n)], scalar=1.0,
                                             in1=o_sum[:], op0=ALU.add, op1=ALU.mult).then_inc(o_s, 1)

                for step, n in STEPS:
                    if step == "unit":
                        unit(n)
                    elif step == "scores":
                        softmax(n)
                        normalise(n)
                    elif step == "turn":
                        for kb in range(1 if n == 0 else 0, 2):
                            dve.wait_ge(pt_hi_s, k * NTURN + (turned(n, kb) + 1))
                            dve.tensor_tensor(pt_lo[:, kb], ps[:, TURN + kb, :], fp(pt_hi[:, kb]),
                                              ALU.subtract).then_inc(pt_lo_s, 1)
                    else:
                        gate_attention(n)
                soft_done(NB - 1, SOFT)
                conv_done(1, 12)
                dve.wait_ge(o_s, k * (3 * NB) + 3 * NB)

            def mixer_low(h, m):
                dve.wait_ge(m_hi_s, DT * h + m + 1)
                dve.scalar_tensor_tensor(out=m_lo[h][:, m], in0=res[:, m, half(h)], scalar=0.5,
                                         in1=fp(m_hi[h][:, m]), op0=ALU.mult, op1=ALU.subtract).then_inc(m_lo_s, 1)

            def x_sum(h, m):
                dve.wait_ge(m_lo_s, DT * h + m + 1)
                dve.tensor_tensor(res[:, m, half(h)], fp(act_hi[:, m, half(h)]), fp(act_lo[:, m, half(h)]),
                                  ALU.add).then_inc(xsum_s, 1)

            def centre(q):
                def odd_squares(m):
                    dve.wait_ge(sq_s, 8 * q + m + 1)
                    if m > 3:
                        dve.wait_ge(odd_s, 3 * q + m // 2 - 1)
                    dve.tensor_tensor(sq_acc[:, 1], sq_acc[:, 1], sq[:, 1], ALU.add).then_inc(odd_s, 1)

                dve.wait_ge(stat_s, 3 * q + 1)
                for m in range(DT):
                    tile = res[:, m, half(q)]
                    dve.tensor_tensor(tile, tile, ps[:, MEAN, :], ALU.subtract).then_inc(cen_s, 1)
                    if m == 5:
                        odd_squares(3)
                odd_squares(5)
                odd_squares(7)

            def invert(q):
                dve.wait_ge(std_s, q + 1)
                dve.reciprocal(inv[:], std[:]).then_inc(inv_s, 1)

            def norm_low(q, m):
                dve.wait_ge(n_hi_s, 8 * q + m + 1)
                dve.scalar_tensor_tensor(out=act_lo[:, m, half(q)], in0=res[:, m, half(q)], scalar=lnb[:, m:m + 1],
                                         in1=fp(act_hi[:, m, half(q)]), op0=ALU.add,
                                         op1=ALU.subtract).then_inc(n_lo_s, 1)

            def normalise_half(q, ms):
                dve.wait_ge(stat_s, 3 * q + 3)
                dve.wait_ge(sq_s, 8 * q + 8)
                for m in ms:
                    tile = res[:, m, half(q)]
                    dve.scalar_tensor_tensor(out=tile, in0=tile, scalar=lng[:, m:m + 1], in1=ps[:, INV, :],
                                             op0=ALU.mult, op1=ALU.mult).then_inc(norm_s, 1)
                    if m > ms[0]:
                        norm_low(q, m - 1)
                norm_low(q, ms[-1])

            def scale_residual(q):
                dve.wait_ge(n_lo_s, 8 * q + 8)
                for m in range(DT):
                    dve.tensor_scalar(res[:, m, half(q)], res[:, m, half(q)], lnb[:, m:m + 1], ALPHA,
                                      ALU.add, ALU.mult).then_inc(scaled_s, 1)

            dve.memset(inv[:], 0.0).then_inc(res_s, OB)
            for m in range(DT):
                mixer_low(0, m)
            for v in range(OUT_TILES):
                h, m = v // DT, v % DT
                if h == 0:
                    x_sum(0, m)
                dve.wait_ge(out_s, v + 1)
                dve.wait_ge(xsum_s, DT * 2 if h else 2 * m + 1)
                dve.scalar_tensor_tensor(out=res[:, m, half(h)], in0=res[:, m, half(h)], scalar=ALPHA,
                                         in1=ps[:, v % OB, :], op0=ALU.mult, op1=ALU.add).then_inc(res_s, 1)
                if h == 0:
                    mixer_low(1, m)
                    x_sum(1, m)
                if v == DT + 1:
                    dve.wait_ge(res_s, OB + DT)
                    centre(0)
                if v == DT + 3:
                    invert(0)
                if v in (DT + 4, DT + 5):
                    normalise_half(0, range(4 * (v - DT - 4), 4 * (v - DT - 3)))
                if v == DT + 6:
                    scale_residual(0)

            def hidden(g, h, t):
                dve.wait_ge(silu_s, g * 8 + (4 * h + 2 * t + 1))
                if h:
                    dve.wait_ge(hid_s, g * 12 + (3 * t + 3))
                dve.scalar_tensor_tensor(out=hid[:, t], in0=tanh_g[:, t], scalar=1.0, in1=ps[:, 2 * t, :],
                                         op0=ALU.add, op1=ALU.mult).then_inc(hid_s, 1)
                dve.wait_ge(f_s, g * 8 + (4 * h + 2 * t + 2))
                dve.wait_ge(hid_s, g * 12 + (6 * h + 3 * t + 1))
                dve.tensor_tensor(hid[:, t], hid[:, t], ps[:, 2 * t + 1, :], ALU.mult).then_inc(hid_s, 1)
                dve.wait_ge(silu_s, g * 8 + (4 * h + 2 * t + 2))
                dve.scalar_tensor_tensor(out=hid_lo[:, t, half(h)], in0=hid[:, t], scalar=0.5,
                                         in1=fp(hid_hi[:, t, half(h)]), op0=ALU.mult,
                                         op1=ALU.subtract).then_inc(hid_s, 1)

            dve.wait_ge(res_s, OB + OUT_TILES)
            centre(1)
            hidden(0, 0, 0)
            invert(1)
            normalise_half(1, range(DT))
            hidden(0, 0, 1)
            scale_residual(1)
            dve.wait_ge(scaled_s, 2 * DT)

            def add_down(g, v):
                h, m = v // DT, v % DT
                dve.wait_ge(d_s, g * 16 + (v + 1))
                dve.tensor_tensor(res[:, m, half(h)], res[:, m, half(h)], ps[:, 4 + v % 4, :],
                                  ALU.add).then_inc(add_s, 1)

            with dve.Fori(0, NG - 1) as g:
                hidden(g, 1, 0)
                hidden(g, 1, 1)
                for v in range(2 * DT):
                    add_down(g, v)
                dve.wait_ge(add_s, g * 16 + 16)
                dve.wait_ge(hid_s, g * 12 + 12)
                hidden(g + 1, 0, 0)
                hidden(g + 1, 0, 1)
            def row_stats(i):
                k = i % 2
                for b in range(2):
                    dve.wait_ge(ot_s, 2 * i + b + 1)
                    dve.bn_stats(bn[:, k, b], row_banks(i)[:, b]).then_inc(bn_s, 1)
                dve.wait_ge(bn_s, 4 * i + 2)
                dve.bn_aggr(mv[:, k], bn[:, k].rearrange("p b s -> p (b s)")).then_inc(bn_s, 1)
                dve.wait_ge(bn_s, 4 * i + 3)
                dve.tensor_scalar(neg_mean[:, k:k + 1], mv[:, k, 0:1], -1.0, None, ALU.mult).then_inc(bn_s, 1)

            def row_scale(i):
                k = i % 2
                dve.wait_ge(std2_s, i + 1)
                dve.reciprocal(inv2[:, k:k + 1], std2[:, k:k + 1]).then_inc(inv2_s, 1)
                dve.wait_ge(inv2_s, i + 1)
                for b in range(1 if i < NB - 1 else 2):
                    cols = slice(0, D) if i < NB - 1 else half(b)
                    dve.wait_ge(rcen_s, i + b + 1)
                    dve.scalar_tensor_tensor(out=row_out(i)[:, cols], in0=row_out(i)[:, cols],
                                             scalar=inv2[:, k:k + 1], in1=ln2_rows[:, 0, cols], op0=ALU.mult,
                                             op1=ALU.mult).then_inc(rgam_s, 1)

            dve.wait_ge(rows_in, 32)
            for step, n in LAST:
                if step == "silu":
                    hidden(NG - 1, 1, n)
                elif step == "rows":
                    row_stats(n)
                    row_scale(n)
            last = row_out(NB - 1)[:, half(1)]
            dve.wait_ge(rgam_s, NB + 1)
            dve.tensor_tensor(last, last, ln2_rows[:, 1, half(1)], ALU.add).then_inc(last_s, 1)

        @block.tensor
        def _(pe):
            def product(bank, w_h, w_l, a_hi, a_lo, tiles, ready=None):
                for t in range(tiles):
                    if ready is not None:
                        ready(t)
                    pe.matmul(bank, w_h(t), a_hi(t), start=(t == 0), stop=False)
                    pe.matmul(bank, w_h(t), a_lo(t), start=False, stop=False)
                    last = pe.matmul(bank, w_l(t), a_hi(t), start=False, stop=(t == tiles - 1))
                return last

            def project(slot, h, bank, ready=None):
                return product(ps[:, bank, :], lambda t: w_hi[:, slot, t], lambda t: w_lo[:, slot, t],
                               lambda t: act_hi[:, t, half(h)], lambda t: act_lo[:, t, half(h)], DT, ready)

            pe.wait_ge(tables, 2)

            def warm_up(n):
                for _ in range(n):
                    pe.transpose(ps[:, 3, 0:P], ident[:], ident[:])

            def turn_x(i):
                st, cg = i // 2, i % 2
                pe.wait_ge(x_in[st], 16)
                if i >= 4:
                    pe.wait_ge(x_lo_s, i - 3)
                for c in range(4):
                    last = pe.transpose(ps[:, 4 + i % 4, blk(c)], xs[:, st, blk(4 * cg + c)], ident[:])
                last.then_inc(x_turned, 1)

            def turn_v(i):
                pe.wait_ge(v_copied, i + 1)
                if i >= 2:
                    pe.wait_ge(v_kept, 2 * (i - 1))
                for b in range(4):
                    last = pe.transpose(ps[:, 3 + i % 2, blk(b)], yc[:, (i % 2) * HALF + b * P:(i % 2) * HALF + (b + 1) * P],
                                        ident[:])
                last.then_inc(v_turned, 1)

            def weave(at, ready=None):
                def hook(t):
                    if ready is not None:
                        ready(t)
                    if t in at:
                        at[t]()
                return hook

            warm_up(WARM[0])
            for i in range(8):
                turn_x(i)
                if i % 2:
                    warm_up(WARM[1 + i // 2])
            turns = [{4: lambda: turn_x(8), 5: lambda: turn_x(9), 7: lambda: turn_x(10)},
                     {0: lambda: turn_x(11), 2: lambda: turn_x(12), 3: lambda: turn_x(13),
                      5: lambda: turn_x(14), 6: lambda: turn_x(15)}]
            for n, (t, h) in enumerate(PRO_UNITS):
                pe.wait_ge(w_lo_s, t + 1)
                if n >= 3:
                    if n - 3 < 4:
                        pe.wait_ge(v_copied, n - 2)
                    else:
                        pe.wait_ge(k_copied, 4 * (n - 6))
                hook = weave(turns[n] if n < 2 else {},
                             (lambda c: pe.wait_ge(x_lo_s, 7 + c // 4)) if n == 0 else None)
                if n > 0:
                    pe.wait_ge(x_lo_s, 16 if h else 8)
                project(t % 2, h, unit_bank(n + 1), hook).then_inc(unit_s, 1)
                if 1 <= n < 5:
                    turn_v(n - 1)

            pe.wait_ge(k_copied, 8)
            with pe.Fori(0, NKV) as k:
                for step, n in STEPS:
                    if step == "unit":
                        if n % 2 == 0:
                            pe.wait_ge(w_lo_s, k * NT + (PRO_TILES + n // 2 + 1))
                        if n in (1, 2):
                            pe.wait_ge(k_copied, 8 + 4 * n)
                        if n == 2:
                            pe.wait_ge(prep_dve, k * 9 + 1)
                        if n >= 3:
                            pe.wait_ge(*consumed(k, n - 3))
                        project((n // 2) % 2, n % 2, unit_bank(n)).then_inc(unit_s, 1)
                    elif step == "scores":
                        if n == 0:
                            pe.wait_ge(prep_dve, k * 9 + 2)
                            pe.wait_ge(q_lo_s, k * 8 + 8)
                        else:
                            pe.wait_ge(soft_s, k * (SOFT * NB) + (SOFT * (n - 1) + 1))
                        keys = slice(max(n - 1, 0) * P, (n + 1) * P)
                        for g in range(G):
                            dst = scores_ps[:, g, (P if n == 0 else 0):]
                            pe.matmul(dst, q_st[:, g, blk(n)], ks_hi[:, keys], start=True, stop=False)
                            last = pe.matmul(dst, q_st[:, g, blk(n)], ks_lo[:, keys], start=False, stop=True)
                        last.then_inc(scores_s, 1)
                    elif step == "turn":
                        pe.wait_ge(soft_s, k * (SOFT * NB) + (SOFT * n + SOFT))
                        if n:
                            pe.wait_ge(pt_lo_s, k * NTURN + turned(n, 0))
                        for kb in range(1 if n == 0 else 0, 2):
                            for g in range(G):
                                last = pe.transpose(ps[:, TURN + kb, blk(g)], prob[:, g, blk(kb)], ident[:])
                            last.then_inc(turn_s, 1)
                    else:
                        pe.wait_ge(pt_lo_s, k * NTURN + (turned(n, 1) + 1))
                        if n:
                            pe.wait_ge(o_s, k * (3 * NB) + (3 * (n - 1) + 2))
                        kbs = [1] if n == 0 else [0, 1]
                        for kb in kbs:
                            for part in (pt_hi, pt_lo):
                                last = pe.matmul(ps[:, OUT, :], vs[:, n - 1 + kb, :], part[:, kb],
                                                 start=(kb == kbs[0] and part is pt_hi),
                                                 stop=(kb == 1 and part is pt_lo))
                        last.then_inc(values_s, 1)
                pe.wait_ge(gc_s, k * 4 + 4)
                pe.wait_ge(conv_s, k * 24 + 23)
                pe.wait_ge(o_s, k * (3 * NB) + (3 * NB - 1))

            def mean(q):
                pe.wait_ge(acc_s, 7 * (q + 1))
                pe.matmul(ps[:, MEAN, :], mean_of[:], acc[:], start=True, stop=True).then_inc(stat_s, 1)

            def variance(q):
                pe.wait_ge(even_s, 3 * (q + 1))
                pe.wait_ge(odd_s, 3 * (q + 1))
                for b in range(4):
                    for part in range(2):
                        last = pe.matmul(ps[:, VAR, b:b + 1], sq_acc[:, part, blk(b)], mean_of[:, 0:1],
                                         start=(part == 0), stop=(part == 1))
                last.then_inc(stat_s, 1)

            def spread(q):
                pe.wait_ge(inv_s, q + 1)
                for b in range(4):
                    last = pe.matmul(ps[:, INV, blk(b)], inv[:, b:b + 1].broadcast_to([P, P]), ident[:],
                                     start=True, stop=True)
                last.then_inc(stat_s, 1)

            def project_out(h, v, w, bank, at={}):
                pe.wait_ge(w_lo_s, v + (IN_TILES + 1))
                pe.wait_ge(res_s, v + 1)
                return product(ps[:, bank, :], lambda t: out_hi(w)[:, t], lambda t: out_lo(w)[:, t],
                               lambda t: m_hi[h][:, t], lambda t: m_lo[h][:, t], DT,
                               weave(at, lambda t: pe.wait_ge(m_lo_s, DT * h + t + 1))).then_inc(out_s, 1)

            with pe.Fori(0, DT // OB) as i:
                for e in range(OB):
                    project_out(0, i * OB + e, e, e)
            for v in range(DT, 2 * DT):
                project_out(1, v, v, v % OB, {DT + 1: {0: lambda: mean(0)}, DT + 3: {7: lambda: variance(0)},
                                              DT + 4: {4: lambda: spread(0)}}.get(v, {}))

            def gate_up(g, h, s, ready=None):
                if h == 0:
                    pe.wait_ge(fw_lo_s, g * 6 + (s + 1))
                w_h, w_l = ffn_hi(s), ffn_lo(s)
                product(ps[:, s, :], lambda t: w_h[:, t], lambda t: w_l[:, t],
                        lambda t: act_hi[:, t, half(h)], lambda t: act_lo[:, t, half(h)], DT,
                        ready).then_inc(f_s, 1)

            def down(g, h, m):
                v = h * DT + m
                if m == 0:
                    pe.wait_ge(fw_lo_s, g * 6 + 6)
                    pe.wait_ge(hid_s, g * 12 + 6 * (h + 1))
                if v >= 4:
                    pe.wait_ge(add_s, g * 16 + (v - 3))
                product(ps[:, 4 + v % 4, :], lambda t: wd_hi[:, t, blk(m)], lambda t: wd_lo[:, t, blk(m)],
                        lambda t: hid_hi[:, t, half(h)], lambda t: hid_lo[:, t, half(h)], 2).then_inc(d_s, 1)

            head_hooks = {0: {5: lambda: mean(1)}, 2: {1: lambda: variance(1), 6: lambda: spread(1)}}
            for s in range(4):
                pe.wait_ge(res_s, OUT_TILES + s + 1)
                gate_up(0, 0, s, weave(head_hooks.get(s, {}),
                                       (lambda t: pe.wait_ge(n_lo_s, t + 1)) if s == 0 else None))

            def second_half(g, s):
                pe.wait_ge(hid_s, g * 12 + (3 * (s // 2) + 1 + s % 2))
                gate_up(g, 1, s, (lambda t: pe.wait_ge(n_lo_s, DT + t + 1)) if s == 0 else None)

            with pe.Fori(0, NG - 1) as g:
                for s in range(4):
                    second_half(g, s)
                for h in range(2):
                    for m in range(DT):
                        down(g, h, m)
                for s in range(4):
                    pe.wait_ge(hid_s, g * 12 + (6 + 3 * (s // 2) + 1 + s % 2))
                    gate_up(g + 1, 0, s)
                pe.wait_ge(add_s, g * 16 + 2 * DT)

            def last_rows(i):
                g = NG - 1
                pe.wait_ge(hid_s, g * 12 + 6 * (i // 4 + 1))
                if i == 0:
                    pe.wait_ge(fw_lo_s, g * 6 + 6)
                if ROW_BANKS[i] in ROW_BANKS[:i]:
                    pe.wait_ge(rcen_s, max(j for j in range(i) if ROW_BANKS[j] == ROW_BANKS[i]) + 1)
                for b in range(2):
                    bank = row_banks(i)[:, b]
                    for c in range(4):
                        pe.matmul(bank[:, blk(c)], res[:, 4 * b + c, blk(i)], ident[:], is_transpose=True,
                                  start=(c == 0), stop=False)
                    for t in range(2):
                        pe.matmul(bank, hid_hi[:, t, blk(i)], wd_hi[:, t, half(b)], start=False, stop=False)
                        pe.matmul(bank, hid_hi[:, t, blk(i)], wd_lo[:, t, half(b)], start=False, stop=False)
                        last = pe.matmul(bank, hid_lo[:, t, blk(i)], wd_hi[:, t, half(b)], start=False, stop=(t == 1))
                    last.then_inc(ot_s, 1)

            for step, n in LAST:
                if step == "unit":
                    second_half(NG - 1, n)
                elif step == "rows":
                    last_rows(n)


_INS = ["x", "w_in", "conv_w", "attn_sinks", "w_out", "ln1_g", "ln1_b", "w_gate", "w_up", "w_down", "ln2_g", "ln2_b"]


def kernel(**inputs):
    import concourse.bacc as bacc
    from concourse.bass_utils import run_bass_kernel_spmd

    nc = bacc.Bacc("TRN2", target_bir_lowering=False, num_devices=1)
    arrays, args = {}, []
    for name in _INS:
        a = np.ascontiguousarray(inputs[name])
        arrays[f"in_{name}"] = a
        args.append(nc.dram_tensor(f"in_{name}", a.shape, mybir.dt.from_np(a.dtype), kind="ExternalInput").ap())
    out = nc.dram_tensor("out", (1, S, D), F32, kind="ExternalOutput").ap()
    build(nc, *args, out)
    r = run_bass_kernel_spmd(nc, [arrays], core_ids=[0])
    return r.results[0]["out"]
```
